# Optimizing a Trainium2 kernel written in Bass

```python
import jax, jax.numpy as jnp
from jax import lax
import numpy as np

D_MODEL = 1024
BATCH = 1
SEQ = 512
DEPTH = 2

CHUNK = 64
D_MIX = D_MODEL
HEAD_DIM = 64
N_Q_HEADS = 8
N_KV_HEADS = 2
GQA_GROUP = N_Q_HEADS // N_KV_HEADS
D_ATTN = N_Q_HEADS * HEAD_DIM
D_KV = N_KV_HEADS * HEAD_DIM
WINDOW = 128
WINDOW_CHUNKS = WINDOW // CHUNK
ROPE_THETA = 10000.0
D_LRU = D_MIX - D_ATTN
LRU_BLOCKS = 8
LRU_BLOCK_DIM = D_LRU // LRU_BLOCKS
LRU_CONV_WIDTH = 4
LRU_C = 8.0
D_IN_PROJ = D_ATTN + 2 * D_KV + 2 * D_LRU
D_FF = 3 * D_MODEL
FFN_CONV_WIDTH = 3
N_MOD = 6
NORM_EPS = 1e-6
MASK_VALUE = -1e30

kernel_name = "hybrid_swa_sink_rglru_convffn_sandwich_adaln"

def rms_norm(x, g):
    x32 = x.astype(jnp.float32)
    y = x32 * lax.rsqrt(jnp.mean(x32 * x32, axis=-1, keepdims=True) + NORM_EPS)
    return (y * g.astype(jnp.float32)).astype(x.dtype)

def causal_dwconv(x, w, b):
    k_width = w.shape[0]
    seq = x.shape[1]
    xp = jnp.pad(x, ((0, 0), (k_width - 1, 0), (0, 0)))
    y = b
    for j in range(k_width):
        y = y + w[j] * xp[:, j:j + seq]
    return y

def rope_tables(positions):
    inv_freq = ROPE_THETA ** (-jnp.arange(0, HEAD_DIM, 2, dtype=jnp.float32) / HEAD_DIM)
    ang = positions.astype(jnp.float32)[..., None] * inv_freq
    return jnp.cos(ang)[:, :, None, :], jnp.sin(ang)[:, :, None, :]

def apply_rope(t, cos, sin):
    t32 = t.astype(jnp.float32)
    t1, t2 = t32[..., :HEAD_DIM // 2], t32[..., HEAD_DIM // 2:]
    return jnp.concatenate([t1 * cos - t2 * sin, t2 * cos + t1 * sin], axis=-1).astype(t.dtype)

def band_chunks(t):
    n_chunks = t.shape[1]
    parts = []
    for j in range(WINDOW_CHUNKS - 1, -1, -1):
        parts.append(jnp.pad(t, ((0, 0), (j, 0), (0, 0), (0, 0), (0, 0)))[:, :n_chunks])
    return jnp.concatenate(parts, axis=2)

def sliding_window_attention(q, k, v, sinks):
    bsz, seq = q.shape[0], q.shape[1]
    n_chunks = seq // CHUNK
    qc = q.reshape(bsz, n_chunks, CHUNK, N_KV_HEADS, GQA_GROUP, HEAD_DIM)
    kb = band_chunks(k.reshape(bsz, n_chunks, CHUNK, N_KV_HEADS, HEAD_DIM))
    vb = band_chunks(v.reshape(bsz, n_chunks, CHUNK, N_KV_HEADS, HEAD_DIM))
    scores = jnp.einsum('bnqhgd,bnkhd->bnhgqk', qc, kb,
                        preferred_element_type=jnp.float32) * (HEAD_DIM ** -0.5)
    chunk_ids = jnp.arange(n_chunks)[:, None]
    key_back = (WINDOW_CHUNKS - 1) - jnp.arange(WINDOW_CHUNKS * CHUNK) // CHUNK
    valid = (chunk_ids - key_back[None, :]) >= 0
    scores = jnp.where(valid[None, :, None, None, None, :], scores, MASK_VALUE)
    sink = jnp.broadcast_to(sinks.astype(jnp.float32).reshape(1, 1, N_KV_HEADS, GQA_GROUP, 1, 1),
                            scores.shape[:-1] + (1,))
    probs = jax.nn.softmax(jnp.concatenate([scores, sink], axis=-1), axis=-1)[..., :-1]
    out = jnp.einsum('bnhgqk,bnkhd->bnqhgd', probs.astype(v.dtype), vb)
    return out.reshape(bsz, seq, D_ATTN)

def rg_lru(x, w_a, b_a, w_x, b_x, lam):
    bsz, seq = x.shape[0], x.shape[1]
    xb = x.reshape(bsz, seq, LRU_BLOCKS, LRU_BLOCK_DIM)
    r = jax.nn.sigmoid((jnp.einsum('bsnd,nde->bsne', xb, w_a).reshape(bsz, seq, D_LRU) + b_a).astype(jnp.float32))
    i = jax.nn.sigmoid((jnp.einsum('bsnd,nde->bsne', xb, w_x).reshape(bsz, seq, D_LRU) + b_x).astype(jnp.float32))
    log_a = -LRU_C * r * jax.nn.softplus(-lam.astype(jnp.float32))
    a = jnp.exp(log_a)
    b = jnp.sqrt(-jnp.expm1(2.0 * log_a)) * (i * x.astype(jnp.float32))

    def combine(left, right):
        a_l, b_l = left
        a_r, b_r = right
        return a_l * a_r, a_r * b_l + b_r

    _, h = lax.associative_scan(combine, (a, b), axis=1)
    return h.astype(x.dtype)

def hybrid_mixer(h, cos, sin, w_in, sinks, conv_w, conv_b, w_a, b_a, w_x, b_x, lam,
                 g_attn, g_lru, w_out):
    bsz, seq = h.shape[0], h.shape[1]
    proj = h @ w_in
    q, k, v, x_lru, gate = jnp.split(
        proj, [D_ATTN, D_ATTN + D_KV, D_ATTN + 2 * D_KV, D_ATTN + 2 * D_KV + D_LRU], axis=-1)
    q = apply_rope(q.reshape(bsz, seq, N_Q_HEADS, HEAD_DIM), cos, sin)
    k = apply_rope(k.reshape(bsz, seq, N_KV_HEADS, HEAD_DIM), cos, sin)
    v = v.reshape(bsz, seq, N_KV_HEADS, HEAD_DIM)
    attn_out = sliding_window_attention(q, k, v, sinks)
    lru_out = rg_lru(causal_dwconv(x_lru, conv_w, conv_b), w_a, b_a, w_x, b_x, lam) \
        * jax.nn.gelu(gate, approximate=True)
    merged = jnp.concatenate([rms_norm(attn_out, g_attn), rms_norm(lru_out, g_lru)], axis=-1)
    return merged @ w_out

def conv_ffn(h, w_up, conv_w, conv_b, w_down):
    u = causal_dwconv(h @ w_up, conv_w, conv_b)
    g, val = jnp.split(u, 2, axis=-1)
    return (jax.nn.gelu(g, approximate=True) * val) @ w_down

def setup_inputs(seed: int = 0) -> dict:
    key = jax.random.key(seed)
    ks = jax.random.split(key, 26)

    def nrm(k, shape, scale):
        return jax.random.normal(k, shape, jnp.float32) * scale

    def gain(k, shape):
        return 1.0 + 0.02 * jax.random.normal(k, shape, jnp.float32)

    x = nrm(ks[0], (BATCH, SEQ, D_MODEL), 1.0)
    c = nrm(ks[1], (BATCH, D_MODEL), 1.0)
    offset = jax.random.randint(ks[2], (BATCH, 1), 0, 8192, dtype=jnp.int32)
    positions = (offset + jnp.arange(SEQ, dtype=jnp.int32)[None, :]).astype(jnp.int32)
    a8 = jax.random.uniform(ks[15], (DEPTH, D_LRU), jnp.float32, minval=0.9, maxval=0.999)
    a0 = a8 ** (1.0 / LRU_C)
    lru_lambda = jnp.log(a0) - jnp.log1p(-a0)
    return {
        "x": x,
        "c": c,
        "positions": positions,
        "ada_w": nrm(ks[3], (DEPTH, D_MODEL, N_MOD * D_MODEL), 0.5 * D_MODEL ** -0.5),
        "ada_b": nrm(ks[4], (DEPTH, N_MOD * D_MODEL), 0.02),
        "mix_pre_g": gain(ks[5], (DEPTH, D_MODEL)),
        "mix_post_g": gain(ks[6], (DEPTH, D_MODEL)),
        "w_in": nrm(ks[7], (DEPTH, D_MODEL, D_IN_PROJ), D_MODEL ** -0.5),
        "attn_sinks": nrm(ks[8], (DEPTH, N_Q_HEADS), 0.5),
        "lru_conv_w": nrm(ks[9], (DEPTH, LRU_CONV_WIDTH, D_LRU), LRU_CONV_WIDTH ** -0.5),
        "lru_conv_b": nrm(ks[10], (DEPTH, D_LRU), 0.01),
        "lru_w_a": nrm(ks[11], (DEPTH, LRU_BLOCKS, LRU_BLOCK_DIM, LRU_BLOCK_DIM), LRU_BLOCK_DIM ** -0.5),
        "lru_b_a": nrm(ks[12], (DEPTH, D_LRU), 0.01),
        "lru_w_x": nrm(ks[13], (DEPTH, LRU_BLOCKS, LRU_BLOCK_DIM, LRU_BLOCK_DIM), LRU_BLOCK_DIM ** -0.5),
        "lru_b_x": nrm(ks[14], (DEPTH, D_LRU), 0.01),
        "lru_lambda": lru_lambda,
        "grp_g_attn": gain(ks[16], (DEPTH, D_ATTN)),
        "grp_g_lru": gain(ks[17], (DEPTH, D_LRU)),
        "w_out": nrm(ks[18], (DEPTH, D_MIX, D_MODEL), D_MIX ** -0.5),
        "ffn_pre_g": gain(ks[19], (DEPTH, D_MODEL)),
        "ffn_post_g": gain(ks[20], (DEPTH, D_MODEL)),
        "ffn_w_up": nrm(ks[21], (DEPTH, D_MODEL, 2 * D_FF), D_MODEL ** -0.5),
        "ffn_conv_w": nrm(ks[22], (DEPTH, FFN_CONV_WIDTH, 2 * D_FF), FFN_CONV_WIDTH ** -0.5),
        "ffn_conv_b": nrm(ks[23], (DEPTH, 2 * D_FF), 0.01),
        "ffn_w_down": nrm(ks[24], (DEPTH, D_FF, D_MODEL), D_FF ** -0.5),
    }

def reference(x, c, positions, ada_w, ada_b, mix_pre_g, mix_post_g, w_in, attn_sinks,
              lru_conv_w, lru_conv_b, lru_w_a, lru_b_a, lru_w_x, lru_b_x, lru_lambda,
              grp_g_attn, grp_g_lru, w_out, ffn_pre_g, ffn_post_g, ffn_w_up, ffn_conv_w,
              ffn_conv_b, ffn_w_down):
    cos, sin = rope_tables(positions)
    c_act = jax.nn.silu(c)
    bsz = c.shape[0]
    for l in range(DEPTH):
        mod = (c_act @ ada_w[l] + ada_b[l]).reshape(bsz, N_MOD, D_MODEL)[:, :, None, :]
        shift_m, scale_m, gate_m = mod[:, 0], mod[:, 1], mod[:, 2]
        shift_f, scale_f, gate_f = mod[:, 3], mod[:, 4], mod[:, 5]
        h = rms_norm(x, mix_pre_g[l]) * (1.0 + scale_m) + shift_m
        y = hybrid_mixer(h, cos, sin, w_in[l], attn_sinks[l], lru_conv_w[l], lru_conv_b[l],
                         lru_w_a[l], lru_b_a[l], lru_w_x[l], lru_b_x[l], lru_lambda[l],
                         grp_g_attn[l], grp_g_lru[l], w_out[l])
        x = x + gate_m * rms_norm(y, mix_post_g[l])
        h = rms_norm(x, ffn_pre_g[l]) * (1.0 + scale_f) + shift_f
        y = conv_ffn(h, ffn_w_up[l], ffn_conv_w[l], ffn_conv_b[l], ffn_w_down[l])
        x = x + gate_f * rms_norm(y, ffn_post_g[l])
    return x


_drawn_inputs = setup_inputs


def setup_inputs(seed=0):
    import zlib

    import numpy as np

    out = dict(_drawn_inputs(seed))
    spreads = {}
    factors = {'mix_pre_g': 6.397,
     'mix_post_g': 6.074,
     'attn_sinks': 8.0,
     'lru_conv_b': 8.0,
     'lru_b_a': 8.0,
     'lru_b_x': 8.0,
     'grp_g_attn': 8.0,
     'grp_g_lru': 8.0,
     'ffn_pre_g': 5.375,
     'ffn_post_g': 7.154,
     'ffn_conv_b': 8.0}
    for name, (base, spread) in spreads.items():
        noise = np.random.default_rng([zlib.crc32(name.encode()), seed]).standard_normal(out[name].shape)
        drawn = base * np.exp(spread * noise) if base else spread * noise
        out[name] = __import__('jax').numpy.asarray(drawn.astype(out[name].dtype))
    for name, factor in factors.items():
        out[name] = (out[name] * factor).astype(out[name].dtype)
    return out
```

```python
import numpy as np
import concourse.bass as bass
from concourse import mybir
from contextlib import ExitStack

P = 128
DEPTH, SEQ, D = 2, 512, 1024
CHUNK, HD, NQ, NKV = 64, 64, 8, 2
D_ATTN, D_LRU = 512, 512
DFF = 3072
EPS = 1e-6
MASK = -1e30
THETA = 10000.0
KT = D // P
AT, LT = D_ATTN // P, D_LRU // P
QT = SEQ // P
PAIRS = DFF // P
GROUPS = PAIRS // KT
PROJ = ["x"] * LT + ["k", "v"] + ["q"] * AT + ["g"] * LT
NPROJ = len(PROJ)
NOUT = KT
GSTEP = 3 * KT
NCH = NPROJ + NOUT + GROUPS * GSTEP
NMOD = 6
CONVW = 4
FCONV = 3
SLOTS = [2 * (s % 4) + s // 4 for s in range(NQ)]

COLS = {}
_at = 0
for _name, _n in [("mix_pre", KT), ("mix_post", KT), ("ffn_pre", KT), ("ffn_post", KT),
                  ("g_attn", AT), ("g_lru", LT), ("lcw", CONVW * LT), ("lcb", LT), ("ba", LT),
                  ("bx", LT), ("lam", LT), ("fcw", FCONV * 2 * PAIRS), ("fcb", 2 * PAIRS),
                  ("ada_b", NMOD * KT), ("sink", NQ)]:
    COLS[_name] = _at
    _at += _n
NPAR = _at

TWO_PI = 6.283185307179586
def _parts(value, bits, n):
    out = []
    for i in range(n):
        if i == n - 1:
            out.append(float(np.float32(value)))
        else:
            q = 2.0 ** (np.floor(np.log2(value)) - bits + 1)
            part = float(np.floor(value / q) * q)
            out.append(part)
            value -= part
    return out
PI_PARTS = _parts(TWO_PI, 11, 3)
ROUND_MAGIC = float(1.5 * 2 ** 23)
COARSE = 1024.0


class Tally:

    def __init__(self, sem):
        self.sem, self.n, self.marks = sem, 0, 0

    def mark(self, instruction):
        instruction.then_inc(self.sem, 1)
        self.n = self.n + 1
        self.marks += 1


def build(nc, A):
    fp32, fp32r, i32 = mybir.dt.float32, mybir.dt.float32r, mybir.dt.int32
    ALU, ACT, AX = mybir.AluOpType, mybir.ActivationFunctionType, mybir.AxisListType
    ctx = ExitStack()
    with ctx:
        def sb(name, shape, dt=fp32):
            return ctx.enter_context(nc.sbuf_tensor("sb_" + name, shape, dt))

        def sem(name):
            return ctx.enter_context(nc.semaphore(name))

        x = sb("x", [P, KT * SEQ])
        hH = sb("hH", [P, KT, SEQ], fp32r)
        hL = sb("hL", [P, KT, SEQ], fp32r)
        mH = sb("mH", [P, KT, SEQ], fp32r)
        mL = sb("mL", [P, KT, SEQ], fp32r)
        y = sb("y", [P, KT * SEQ])
        raw = sb("raw", [P, 2, KT * P])
        wH = sb("wH", [P, 2, KT * P], fp32r)
        wL = sb("wL", [P, 2, KT * P], fp32r)
        adaw = sb("adaw", [P, 4, D])
        macc = sb("macc", [P, D])
        par = sb("par", [P, DEPTH, NPAR])
        mod = sb("mod", [P, DEPTH * NMOD, KT])
        fac = sb("fac", [P, DEPTH, 4, KT])
        gw = sb("gw", [P, 2 * LT, P])
        ones = sb("ones", [P, P])
        ident = sb("ident", [P, P])
        R = sb("R", [P, 4, SEQ])
        I = sb("I", [P, 4, SEQ])
        Adec = sb("Adec", [P, 4, SEQ])
        xc = sb("xc", [P, 4, SEQ])
        kd = sb("kd", [P, NKV, CHUNK + SEQ])
        vw = sb("vw", [P, 8, P])
        scr = sb("scr", [P, 2 * SEQ])
        work = sb("work", [P, 2 * SEQ])
        cosT = sb("cosT", [P, SEQ])
        sinT = sb("sinT", [P, SEQ])
        sq = sb("sq", [P, SEQ])
        ssq = sb("ssq", [P, SEQ])
        tiny = sb("tiny", [P, 96])

        ps = ctx.enter_context(nc.psum_tensor("ps", [P, 8 * SEQ], fp32))

        def bank(b, n=1):
            return ps[:, b * SEQ:(b + n) * SEQ]

        def xt(j):
            return x[:, j * SEQ:(j + 1) * SEQ]

        def yt(j):
            return y[:, j * SEQ:(j + 1) * SEQ]

        vT = y[:, AT * SEQ:AT * SEQ + CHUNK + SEQ]
        Rf = R[:, :, :].rearrange("p a b -> p (a b)")
        scores = [work[:, :], Rf[:, 0:2 * SEQ]]
        probsT = [scr[:, :], Rf[:, 2 * SEQ:4 * SEQ]]
        diag = work[:, 0:SEQ]
        sqb = [sq[:, :], work[:, SEQ:2 * SEQ]]
        NORM_COLS = 7
        MODC = 256

        def pcol(l, name, i=0):
            c = COLS[name] + i
            return par[:, l, c:c + 1]

        mx = [tiny[:, 0:8], tiny[:, 8:16]]
        den = [tiny[:, 16:24], tiny[:, 24:32]]
        es = [tiny[:, 32:40], tiny[:, 40:48]]
        sd = tiny[:, 48:52]
        rs = tiny[:, 52:56]
        eps = tiny[:, 56:57]
        sign = tiny[:, 57:58]
        freq = tiny[:, 58:59]
        zero = tiny[:, 59:60]
        csil = tiny[:, 64:72]
        craw = tiny[:, 72:80]
        ctmp = tiny[:, 80:88]
        spl = sb("spl", [P, DEPTH, LT])
        nspl = sb("nspl", [P, DEPTH, LT])
        sp1 = sb("sp1", [P, DEPTH, LT])
        sp2 = sb("sp2", [P, DEPTH, LT])
        sp3 = sb("sp3", [P, DEPTH, LT])

        w_in = [sem("w_in0"), sem("w_in1")]
        w_hi, w_lo = sem("w_hi"), sem("w_lo")
        chunk_done = sem("chunk_done")
        ada_in = [sem(f"ada_in{i}") for i in range(4)]
        ada_used = sem("ada_used")
        macc_ready, mod_cols, mod_done = sem("macc_ready"), sem("mod_cols"), sem("mod_done")
        params_in, x_in, gw_in, pos_in = sem("params_in"), sem("x_in"), sem("gw_in"), sem("pos_in")
        consts = sem("consts")
        dve_self, act_self = sem("dve_self"), sem("act_self")
        c_exp, c_ready, sp_exp, sp_ready = sem("c_exp"), sem("c_ready"), sem("sp_exp"), sem("sp_ready")
        ang_ready, sin_ready, rope_ready = sem("ang_ready"), sem("sin_ready"), sem("rope_ready")
        ssq_ready, cols_ready, sd_ready = sem("ssq_ready"), sem("cols_ready"), sem("sd_ready")
        diag_ready, rb_ready = sem("diag_ready"), sem("rb_ready")
        sq_ready, sq_used = sem("sq_ready"), sem("sq_used")
        tmp_ready, hi_ready, lo_ready = sem("tmp_ready"), sem("hi_ready"), sem("lo_ready")
        x_done = sem("x_done")
        x_base, acc_dve, acc_act = sem("x_base"), sem("acc_dve"), sem("acc_act")
        swap_ready, v_pad = sem("swap_ready"), sem("v_pad")
        gate_mm, sig_done, aT_ready, b2_ready = sem("gate_mm"), sem("sig_done"), sem("aT_ready"), sem("b2_ready")
        root_ready = sem("root_ready")
        vw_mm, vw_ready = sem("vw_mm"), sem("vw_ready")
        s_mm, s_copied, s_sub, s_exp, p_ready = sem("s_mm"), sem("s_copied"), sem("s_sub"), sem("s_exp"), sem("p_ready")
        pt_mm, pt_copied, o_mm, o_copied, osq_ready = sem("pt_mm"), sem("pt_copied"), sem("o_mm"), sem("o_copied"), sem("osq_ready")
        gelu_ready, l_ready, lsq_ready = sem("gelu_ready"), sem("l_ready"), sem("lsq_ready")
        out_copied = sem("out_copied")
        f_base, f_taps, f_gelu, f_mul = sem("f_base"), sem("f_taps"), sem("f_gelu"), sem("f_mul")
        act_hi, act_lo, dn_read = sem("act_hi"), sem("act_lo"), sem("dn_read")
        stored = sem("stored")
        block = ctx.enter_context(nc.Block())

        NORMS = 6
        def norm_no(l, k):
            return 1 + l * NORMS + k
        RB_BANK = [2, 3, 4, 5, 6, 2]
        def conv_no(l, k):
            return KT + l * 3 * KT + k * KT
        def sq_no(l, k):
            return KT + l * 4 * KT + k * KT

        def proj_release(l, i):
            dve_kinds = "xkq"
            if PROJ[i] in dve_kinds:
                per = sum(k in dve_kinds for k in PROJ)
                return acc_dve, l * per + sum(k in dve_kinds for k in PROJ[:i + 1])
            per = sum(k not in dve_kinds for k in PROJ)
            return acc_act, l * per + sum(k not in dve_kinds for k in PROJ[:i + 1])

        MAC_STEPS = {0: {0: [0], 1: [1], 2: [2], 3: [3], 4: [4], 5: [5, 6], 6: [7],
                         7: [8], 8: [9], 9: [10, 11], 10: [12], 11: [13], 12: [14], 13: [15],
                         14: [16], 15: [17], 16: [18], 17: [19], 18: [20], 19: [21], 20: [22], 21: [23]},
                     1: {14 + i: [i] for i in range(8)}}
        MAC_FIRST = {0: 2 * KT, 1: 11 * KT}
        MOD_AT = {0: {8: 2, 15: 3, 21: 4}, 1: {21: 11}}

        def step_base(l):
            return l * NCH

        @block.sync
        def _(sp):
            sp.dma_start(par[:, :, :], A["par"].rearrange("l p c -> p l c")).then_inc(params_in, 16)
            sp.dma_start(craw, A["c"]).then_inc(params_in, 16)
            sp.dma_start(freq, A["inv_freq"]).then_inc(params_in, 16)
            sp.dma_start(x[:, :], A["x"]).then_inc(x_in, 16)
            sp.dma_start(Adec[:, 0, :].bitcast(i32), A["pos"]).then_inc(pos_in, 16)
            sp.dma_start(gw[:, :, :], A["gw"][0]).then_inc(gw_in, 16)
            stream = A["w"]
            for s in range(2):
                sp.dma_start(raw[:, s, :], stream[s]).then_inc(w_in[s], 16)
            with sp.Fori(0, DEPTH * NCH // 2 - 1) as i:
                for s in range(2):
                    sp.wait_ge(w_lo, i * 2 + s + 1)
                    sp.dma_start(raw[:, s, :], stream[bass.ds(i * 2 + s + 2, 1)]
                                 .rearrange("a p c -> p (a c)")).then_inc(w_in[s], 16)
            for j in range(KT):
                sp.wait_ge(x_done, (2 * DEPTH - 1) * KT + j + 1)
                sp.dma_start(A["out"][:, j * SEQ:(j + 1) * SEQ], xt(j)).then_inc(stored, 16)
            sp.wait_ge(stored, 16 * KT)

        @block.gpsimd
        def _(pool):
            made = 0

            def const(tile, value):
                nonlocal made
                nc.gpsimd.memset(tile, value).then_inc(consts, 1)
                made += 1
                pool.wait_ge(consts, made)
            const(ident[:, :], 0.0)
            const(ones[:, :], 1.0)
            const(eps, EPS)
            const(kd[:, :, 0:CHUNK], 0.0)
            for q4 in range(4):
                const(sign[32 * q4:32 * q4 + 32, :], -1.0 if q4 % 2 == 0 else 1.0)
            nc.gpsimd.affine_select(out=ident[:, :], in_=ident[:, :], compare_op=ALU.not_equal, fill=1.0,
                                    base=0, pattern=[[-1, P]], channel_multiplier=1).then_inc(consts, 1)
            for s in range(4):
                pool.dma_start(adaw[:, s, :], A["ada"][s]).then_inc(ada_in[s], 16)
            with pool.Fori(0, DEPTH * NMOD * KT // 4 - 1) as i:
                for s in range(4):
                    pool.wait_ge(ada_used, i * 4 + s + 1)
                    pool.dma_start(adaw[:, s, :], A["ada"][bass.ds(i * 4 + s + 4, 1)]
                                   .rearrange("a p c -> p (a c)")).then_inc(ada_in[s], 16)
        NCONST = 9

        @block.scalar
        def _(act):
            S = Tally(act_self)

            def self_wait():
                act.wait_ge(act_self, S.n)

            def hi(n, first=False):
                s = n_par(n)
                if not first:
                    act.wait_ge(chunk_done, n - 1)
                act.wait_ge(w_in[s], w_count(n))
                nc.scalar.activation(wH[:, s, :], raw[:, s, :], ACT.Copy).then_inc(w_hi, 1)

            state = {"par": 0}

            def n_par(n):
                return state["par"]

            def w_count(n):
                return state["wc"]

            def split_step(n, parity, first=False):
                state["par"] = parity
                state["wc"] = (n - parity) * 8 + 16
                hi(n, first)

            def sd_step(m, dim):
                act.wait_ge(cols_ready, m + 1)
                nc.scalar.activation(sd, bank(NORM_COLS)[:, 0:QT], ACT.Sqrt, bias=eps,
                                     scale=1.0 / dim).then_inc(sd_ready, 1)

            def squares_of(m0, j, src, wait_sem, wait_value, own=False):
                if not own:
                    act.wait_ge(wait_sem, wait_value)
                if j >= 2:
                    act.wait_ge(sq_used, m0 + j - 1)
                dst = ssq[:, :] if j == 0 else sqb[j % 2]
                nc.scalar.activation(dst, src, ACT.Square).then_inc(sq_ready, 1)

            def hi_tiles(k0, dst, bias):
                for j in range(KT):
                    act.wait_ge(tmp_ready, k0 + j + 1)
                    if bias is None:
                        nc.scalar.activation(dst[:, j, :], yt(j), ACT.Copy).then_inc(hi_ready, 1)
                    else:
                        nc.scalar.activation(dst[:, j, :], yt(j), ACT.Identity,
                                             bias=bias[:, j:j + 1], scale=1.0).then_inc(hi_ready, 1)

            act.wait_ge(params_in, 48)
            nc.scalar.activation(ctmp, craw, ACT.Exp, scale=-1.0).then_inc(c_exp, 1)
            lam = par[:, :, COLS["lam"]:COLS["lam"] + LT]
            S.mark(nc.scalar.activation(sp1[:, :, :], lam, ACT.Abs))
            self_wait()
            nc.scalar.activation(sp2[:, :, :], sp1[:, :, :], ACT.Exp, scale=-1.0).then_inc(sp_exp, 1)
            act.wait_ge(x_in, 16)
            for j in range(KT):
                squares_of(0, j, xt(j), None, None, own=True)
            split_step(0, 0, True)
            split_step(1, 1, True)
            act.wait_ge(ang_ready, 1)
            nc.scalar.activation(sinT[:, :], R[:, 0, :], ACT.Sin).then_inc(sin_ready, 1)
            nc.scalar.activation(cosT[:, :], R[:, 0, :], ACT.Sin, scale=0.5).then_inc(sin_ready, 1)
            sd_step(0, D)
            act.wait_ge(mod_done, 2)
            hi_tiles(0, hH, mod[:, 0, :])

            for l in range(DEPTH):
                B = step_base(l)
                par_l = par[:, l, :]
                for i, kind in enumerate(PROJ):
                    n = B + i
                    split_step(n + 2, n % 2)
                    acc = bank(i % 2)
                    act.wait_ge(chunk_done, n + 1)
                    if kind == "x":
                        nc.scalar.activation(xc[:, i, :], acc, ACT.Identity, bias=pcol(l, "lcb", i),
                                             scale=pcol(l, "lcw", (CONVW - 1) * LT + i)).then_inc(x_base, 1)
                    elif kind in "kq":
                        j = i - LT if kind == "k" else i - LT - 1
                        if kind == "q":
                            rel, val = proj_release(l, i - 1 if PROJ[i - 1] == "q" else LT)
                            act.wait_ge(rel, val)
                        for q4 in range(4):
                            o = q4 ^ 1
                            last = nc.scalar.activation(scr[32 * q4:32 * q4 + 32, 0:SEQ],
                                                        acc[32 * o:32 * o + 32, :], ACT.Copy)
                        last.then_inc(swap_ready, 1)
                    elif kind == "v":
                        act.wait_ge(v_pad, l + 1)
                        nc.scalar.activation(vT[:, CHUNK:], acc, ACT.Copy).then_inc(acc_act, 1)
                    else:
                        j = i - (NPROJ - LT)
                        if j == 0:
                            act.wait_ge(b2_ready, (l + 1) * LT)
                        nc.scalar.activation(xc[:, j, :], acc, ACT.Copy).then_inc(acc_act, 1)
                    if 1 <= i <= LT:
                        j = i - 1
                        act.wait_ge(gate_mm, l * LT + j + 1)
                        b = 2 + 2 * (j % 2)
                        S.mark(nc.scalar.activation(R[:, j, :], bank(b), ACT.Sigmoid, bias=pcol(l, "ba", j)))
                        nc.scalar.activation(I[:, j, :], bank(b + 1), ACT.Sigmoid,
                                             bias=pcol(l, "bx", j)).then_inc(sig_done, 1)
                    if i in (LT + 1, LT + 2):
                        for j in range(2 * (i - LT - 1), 2 * (i - LT - 1) + 2):
                            if j >= 2:
                                act.wait_ge(b2_ready, l * LT + j - 1)
                            self_wait()
                            S.mark(nc.scalar.activation(Adec[:, j, :], R[:, j, :], ACT.Exp,
                                                        scale=nspl[:, l, j:j + 1]))
                            self_wait()
                            nc.scalar.activation(R[:, j, :], R[:, j, :], ACT.Tanh, scale=spl[:, l, j:j + 1])
                            nc.scalar.activation(work[:, (j % 2) * SEQ:(j % 2 + 1) * SEQ], Adec[:, j, :],
                                                 ACT.Square).then_inc(aT_ready, 1)
                    if i == LT + 3:
                        act.wait_ge(b2_ready, (l + 1) * LT)
                        nc.scalar.activation(Rf, Rf, ACT.Sqrt).then_inc(root_ready, 1)
                    if i == LT + 4:
                        act.wait_ge(vw_mm, l + 1)
                        nc.scalar.activation(vw[:, :, :].rearrange("p a b -> p (a b)"), bank(4, 2),
                                             ACT.Copy).then_inc(vw_ready, 1)

                    def copy_scores(t):
                        act.wait_ge(s_mm, l * QT + t + 1)
                        if t >= 2:
                            act.wait_ge(pt_mm, l * QT + t - 1)
                        nc.scalar.activation(scores[t % 2], bank(2, 2), ACT.Copy,
                                             scale=HD ** -0.5).then_inc(s_copied, 1)

                    def exps(t):
                        act.wait_ge(s_sub, l * QT + t + 1)
                        nc.scalar.activation(es[t % 2], es[t % 2], ACT.Exp)
                        nc.scalar.activation(scores[t % 2], scores[t % 2], ACT.Exp).then_inc(s_exp, 1)

                    def copy_pt(t):
                        act.wait_ge(pt_mm, l * QT + t + 1)
                        if t >= 2:
                            act.wait_ge(o_mm, l * QT + t - 1)
                        nc.scalar.activation(probsT[t % 2], bank(4, 2), ACT.Copy).then_inc(pt_copied, 1)

                    def copy_out(t):
                        act.wait_ge(o_mm, l * QT + t + 1)
                        o4 = bank(6).rearrange("p (j q) -> p j q", j=AT)
                        dst = y[:, 0:AT * SEQ].rearrange("p (j q) -> p j q", j=AT)[:, :, t * P:(t + 1) * P]
                        nc.scalar.activation(dst, o4, ACT.Copy)
                        if t >= 1:
                            act.wait_ge(osq_ready, l * QT + t)
                        nc.scalar.activation(sq[:, :], bank(6), ACT.Square).then_inc(o_copied, 1)

                    first_g = NPROJ - LT
                    if i == first_g:
                        copy_scores(0); exps(0)
                    if i == first_g + 1:
                        copy_scores(1); exps(1)
                    if i == first_g + 2:
                        copy_pt(0); copy_scores(2); exps(2)
                    if i == first_g + 3:
                        copy_out(0); copy_pt(1); copy_scores(3); exps(3)
                        copy_out(1); copy_pt(2); copy_out(2); copy_pt(3); copy_out(3)

                xcf = xc[:, :, :].rearrange("p a b -> p (a b)")
                nc.scalar.activation(xcf, xcf, ACT.Gelu_apprx_tanh).then_inc(gelu_ready, 1)
                sd_step(norm_no(l, 0), D_ATTN)
                for j in range(LT):
                    act.wait_ge(l_ready, l * LT + j + 1)
                    nc.scalar.activation(R[:, j, :], yt(AT + j), ACT.Square).then_inc(lsq_ready, 1)
                sd_step(norm_no(l, 1), D_LRU)
                hi_tiles(conv_no(l, 0), mH, None)
                for j in range(NOUT):
                    n = B + NPROJ + j
                    split_step(n + 2, n % 2)
                    act.wait_ge(chunk_done, n + 1)
                    if j == 0:
                        act.wait_ge(lo_ready, conv_no(l, 0) + KT)
                    acc = bank(j % 2)
                    nc.scalar.activation(yt(j), acc, ACT.Copy)
                    if j >= 2:
                        act.wait_ge(sq_used, sq_no(l, 0) + j - 1)
                    dst = ssq[:, :] if j == 0 else sqb[j % 2]
                    nc.scalar.activation(dst, acc, ACT.Square).then_inc(sq_ready, 1)
                sd_step(norm_no(l, 2), D)
                for j in range(KT):
                    squares_of(sq_no(l, 1), j, xt(j), x_done, 2 * l * KT + j + 1)
                sd_step(norm_no(l, 3), D)
                hi_tiles(conv_no(l, 1), hH, mod[:, l * NMOD + 3, :])
                if l + 1 < DEPTH:
                    act.dma_start(gw[:, :, :], A["gw"][l + 1]).then_inc(gw_in, 16)

                for g in range(GROUPS):
                    G = B + NPROJ + NOUT + g * GSTEP
                    U = l * 2 * PAIRS + g * 2 * KT
                    Q = l * PAIRS + g * KT
                    with act.Fori(0, 2) as it:
                        for c in range(8):
                            n = it * 8 + G + c
                            u = it * 8 + U + c
                            pr = it * 4 + Q + c // 2
                            split_step(n + 2, c % 2)
                            if c % 2:
                                act.wait_ge(f_taps, u + 4)
                                nc.scalar.activation(I[:, (c // 2) % 2, :], R[:, (c - 1) % 4, :],
                                                     ACT.Gelu_apprx_tanh).then_inc(f_gelu, 1)
                            act.wait_ge(chunk_done, n + 1)
                            col = it * 4 + (g * KT + c // 2 + (c % 2) * PAIRS)
                            nc.scalar.activation(
                                R[:, c % 4, :], bank(c % 4), ACT.Identity,
                                bias=par_l[:, bass.ds(col + COLS["fcb"], 1)],
                                scale=par_l[:, bass.ds(col + (COLS["fcw"] + 2 * 2 * PAIRS), 1)]).then_inc(f_base, 1)
                            if c % 2:
                                act.wait_ge(f_mul, pr + 1)
                                nc.scalar.activation(mH[:, bass.ds(it * 4 + c // 2, 1), :].rearrange("p a b -> p (a b)"),
                                                     I[:, 2 + (c // 2) % 2, :], ACT.Copy).then_inc(act_hi, 1)
                    last_group = g == GROUPS - 1
                    V = G + 2 * KT
                    if not last_group:
                        with act.Fori(0, KT // 2) as it:
                            for c in range(2):
                                split_step(it * 2 + (V + c + 2), c % 2)
                    else:
                        for j in range(KT):
                            if V + j + 2 < DEPTH * NCH:
                                split_step(V + j + 2, j % 2)
                            squares_of(sq_no(l, 2), j, yt(j), dn_read, l * KT * GROUPS + g * KT + j + 1 + 2)
                sd_step(norm_no(l, 4), D)
                if l + 1 < DEPTH:
                    for j in range(KT):
                        squares_of(sq_no(l, 3), j, xt(j), x_done, (2 * l + 1) * KT + j + 1)
                    sd_step(norm_no(l, 5), D)
                    hi_tiles(conv_no(l, 2), hH, mod[:, (l + 1) * NMOD, :])

        @block.vector
        def _(dve):
            V = Tally(dve_self)
            TT, TS, STT = nc.vector.tensor_tensor, nc.vector.tensor_scalar, nc.vector.scalar_tensor_tensor

            def self_wait():
                dve.wait_ge(dve_self, V.n)

            def link(ins):
                V.mark(ins)
                self_wait()

            def lo_chunk(n, parity):
                dve.wait_ge(w_hi, n + 1)
                TT(wL[:, parity, :], raw[:, parity, :], wH[:, parity, :].bitcast(fp32),
                   ALU.subtract).then_inc(w_lo, 1)

            def mac(u, slot, first, last, count):
                dve.wait_ge(ada_in[slot], count)
                cc = csil
                kt = slot_kt["kt"]
                if first:
                    ins = TS(macc[:, :], adaw[:, slot, :], cc[:, kt:kt + 1], None, ALU.mult)
                else:
                    ins = STT(out=macc[:, :], in0=adaw[:, slot, :], scalar=cc[:, kt:kt + 1], in1=macc[:, :],
                              op0=ALU.mult, op1=ALU.add)
                ins.then_inc(ada_used, 1)
                dve.wait_ge(ada_used, u + 1)
                if last:
                    dve.sem_inc(macc_ready, 1)

            slot_kt = {"kt": 0}

            def mac_unit(seg, kt):
                slot_kt["kt"] = kt
                if kt == 0:
                    if not (isinstance(seg, int) and seg == 0):
                        dve.wait_ge(mod_cols, seg + 0)
                u = seg * KT + kt
                mac(u, kt % 4, kt == 0, kt == KT - 1, (seg * 2 + kt // 4 + 1) * 16)

            def mod_store(seg, l_static, bcol):
                dve.wait_ge(mod_cols, seg + 1)
                out = mod[:, seg, :] if isinstance(seg, int) else mod[:, bass.ds(seg, 1), :].rearrange("p a b -> p (a b)")
                TT(out, bank(NORM_COLS)[:, MODC:MODC + KT], bcol, ALU.add).then_inc(mod_done, 1)
                dve.wait_ge(mod_done, seg + 1)

            def mod_bias(seg):
                l, s = divmod(seg, NMOD)
                c = COLS["ada_b"] + s * KT
                return par[:, l, c:c + KT]

            def factors(l, which):
                seg, gain = [(1, "mix_pre"), (2, "mix_post"), (4, "ffn_pre"), (5, "ffn_post")][which]
                g = par[:, l, COLS[gain]:COLS[gain] + KT]
                m = mod[:, l * NMOD + seg, :]
                if which % 2 == 0:
                    link(STT(out=fac[:, l, which, :], in0=m, scalar=1.0, in1=g, op0=ALU.add, op1=ALU.mult))
                else:
                    link(TT(fac[:, l, which, :], m, g, ALU.mult))

            def make_diag(m):
                dve.wait_ge(sd_ready, m + 1)
                link(nc.vector.reciprocal(rs, sd))
                TT(diag.rearrange("p (t q) -> p t q", t=QT),
                   ident[:, :].unsqueeze(1).broadcast_to([P, QT, P]),
                   rs.unsqueeze(2).broadcast_to([P, QT, P]), ALU.mult).then_inc(diag_ready, 1)

            def add_square(m0, j):
                dve.wait_ge(sq_ready, m0 + j + 1)
                if j > 0:
                    TT(ssq[:, :], ssq[:, :], sqb[j % 2], ALU.add).then_inc(sq_used, 1)
                else:
                    dve.sem_inc(sq_used, 1)
                dve.wait_ge(sq_used, m0 + j + 1)
                if j == KT - 1:
                    dve.sem_inc(ssq_ready, 1)

            def split_tiles(k0, gains, rbs, dst, bias):
                def tmp(j):
                    STT(out=yt(j), in0=src(j), scalar=gains(j), in1=rbs(j), op0=ALU.mult,
                        op1=ALU.mult).then_inc(tmp_ready, 1)
                src = split_src["f"]
                tmp(0)
                for j in range(KT):
                    if j + 1 < KT:
                        tmp(j + 1)
                    dve.wait_ge(hi_ready, k0 + j + 1)
                    if bias is None:
                        TT(dst[:, j, :], yt(j), hi_of(dst)[:, j, :], ALU.subtract).then_inc(lo_ready, 1)
                    else:
                        STT(out=dst[:, j, :], in0=yt(j), scalar=bias[:, j:j + 1],
                            in1=hi_of(dst)[:, j, :], op0=ALU.add, op1=ALU.subtract).then_inc(lo_ready, 1)

            split_src = {"f": xt}

            def hi_of(dst):
                return (hH if dst is hL else mH)[:, :, :].bitcast(fp32)

            dve.sem_inc(f_taps, 4)
            dve.sem_inc(dn_read, 2)
            dve.wait_ge(consts, NCONST)
            dve.wait_ge(params_in, 48)
            dve.wait_ge(c_exp, 1)
            link(TS(ctmp, ctmp, 1.0, None, ALU.add))
            link(nc.vector.reciprocal(ctmp, ctmp))
            link(TT(csil, craw, ctmp, ALU.mult))
            for kt in range(KT):
                mac_unit(0, kt)
            for j in range(KT):
                add_square(0, j)
            lo_chunk(0, 0)
            lo_chunk(1, 1)
            dve.wait_ge(pos_in, 16)
            ang, turns = R[:, 0, :], R[:, 1, :]
            link(nc.vector.tensor_copy(R[:, 2, :], Adec[:, 0, :].bitcast(i32)))
            link(TS(ang, R[:, 2, :], freq, None, ALU.mult))
            for unit in (COARSE, 1.0):
                link(TS(turns, ang, 1.0 / (TWO_PI * unit), ROUND_MAGIC, ALU.mult, ALU.add))
                link(TS(turns, turns, ROUND_MAGIC, None, ALU.subtract))
                for part in PI_PARTS:
                    link(STT(out=ang, in0=turns, scalar=-part * unit, in1=ang, op0=ALU.mult, op1=ALU.add))
            PI = 3.1415925
            link(TS(ang, ang, PI, -PI, ALU.min, ALU.max))
            dve.sem_inc(ang_ready, 1)
            for kt in range(KT):
                mac_unit(1, kt)
            make_diag(0)
            mod_store(0, 0, mod_bias(0))
            mod_store(1, 0, mod_bias(1))
            factors(0, 0)
            dve.wait_ge(rb_ready, 1)
            split_tiles(0, lambda j: fac[:, 0, 0, j:j + 1], lambda j: bank(2), hL, mod[:, 0, :])
            dve.wait_ge(sp_exp, 1)
            lam = par[:, :, COLS["lam"]:COLS["lam"] + LT]
            link(TS(sp1[:, :, :], sp2[:, :, :], 2.0, None, ALU.add))
            link(nc.vector.reciprocal(sp1[:, :, :], sp1[:, :, :]))
            link(TT(sp2[:, :, :], sp2[:, :, :], sp1[:, :, :], ALU.mult))
            link(TT(sp1[:, :, :], sp2[:, :, :], sp2[:, :, :], ALU.mult))
            link(TS(sp3[:, :, :], sp1[:, :, :], 1.0 / 17, None, ALU.mult))
            for k in range(15, 1, -2):
                link(STT(out=sp3[:, :, :], in0=sp3[:, :, :], scalar=1.0 / k, in1=sp1[:, :, :],
                         op0=ALU.add, op1=ALU.mult))
            link(STT(out=sp3[:, :, :], in0=sp3[:, :, :], scalar=1.0, in1=sp2[:, :, :], op0=ALU.add, op1=ALU.mult))
            link(TS(sp1[:, :, :], lam, -1.0, 0.0, ALU.mult, ALU.max))
            link(STT(out=sp3[:, :, :], in0=sp3[:, :, :], scalar=2.0, in1=sp1[:, :, :], op0=ALU.mult, op1=ALU.add))
            link(TS(spl[:, :, :], sp3[:, :, :], 8.0, None, ALU.mult))
            link(TS(nspl[:, :, :], sp3[:, :, :], -8.0, None, ALU.mult))
            dve.sem_inc(sp_ready, 1)
            dve.wait_ge(sin_ready, 2)
            link(TS(sinT[:, :], sinT[:, :], sign, None, ALU.mult))
            link(TT(cosT[:, :], cosT[:, :], cosT[:, :], ALU.mult))
            link(TS(cosT[:, :], cosT[:, :], -2.0, 1.0, ALU.mult, ALU.add))

            for l in range(DEPTH):
                B = step_base(l)
                par_l = par[:, l, :]

                def extra(i):
                    for k in MAC_STEPS[l].get(i, []):
                        seg, kt = divmod(MAC_FIRST[l] + k, KT)
                        mac_unit(seg, kt)
                    if i in MOD_AT[l]:
                        seg = MOD_AT[l][i]
                        mod_store(seg, l, mod_bias(seg))

                def softmax(t):
                    sc = scores[t % 2].rearrange("p (s k) -> p s k", s=NQ)
                    m8, e8, d8 = mx[t % 2], es[t % 2], den[t % 2]
                    bc = lambda v: v.unsqueeze(2).broadcast_to([P, NQ, P])
                    sink = par_l[:, COLS["sink"]:COLS["sink"] + NQ]
                    dve.wait_ge(s_copied, l * QT + t + 1)
                    if t == 0:
                        link(nc.vector.memset(sc[0:CHUNK, :, 0:CHUNK], MASK))
                    link(nc.vector.tensor_reduce(m8, sc, AX.X, ALU.max))
                    link(TT(m8, m8, sink, ALU.max))
                    TT(e8, sink, m8, ALU.subtract)
                    TT(sc, sc, bc(m8), ALU.subtract).then_inc(s_sub, 1)
                    dve.wait_ge(s_exp, l * QT + t + 1)
                    link(nc.vector.tensor_reduce(d8, sc, AX.X, ALU.add))
                    link(TT(d8, d8, e8, ALU.add))
                    link(nc.vector.reciprocal(d8, d8))
                    TT(sc, sc, bc(d8), ALU.mult).then_inc(p_ready, 1)

                def out_squares(t):
                    dve.wait_ge(o_copied, l * QT + t + 1)
                    nc.vector.tensor_reduce(ssq[:, t * P:(t + 1) * P],
                                            sq[:, :].rearrange("p (j q) -> p q j", j=AT),
                                            AX.X, ALU.add).then_inc(osq_ready, 1)

                for i, kind in enumerate(PROJ):
                    n = B + i
                    lo_chunk(n + 2, n % 2)
                    acc = bank(i % 2)
                    if kind == "x":
                        dve.wait_ge(x_base, l * LT + i + 1)
                        for k in range(CONVW - 2, -1, -1):
                            back = CONVW - 1 - k
                            ins = STT(out=xc[:, i, back:], in0=acc[:, 0:SEQ - back],
                                      scalar=pcol(l, "lcw", k * LT + i), in1=xc[:, i, back:],
                                      op0=ALU.mult, op1=ALU.add)
                            if k:
                                link(ins)
                        ins.then_inc(acc_dve, 1)
                    elif kind in "kq":
                        j = 0 if kind == "k" else i - LT - 1
                        dve.wait_ge(swap_ready, l * (AT + 1) + j + 1)
                        t1, t2 = scr[:, SEQ:2 * SEQ], scr[:, 0:SEQ]
                        V.mark(TT(t1, acc, cosT[:, :], ALU.mult))
                        link(TT(t2, t2, sinT[:, :], ALU.mult))
                        if kind == "q":
                            TT(yt(i - LT - 2), t1, t2, ALU.add).then_inc(acc_dve, 1)
                        else:
                            V.mark(TT(kd[0:HD, 0, CHUNK:], t1[0:HD], t2[0:HD], ALU.add))
                            link(TT(kd[HD:P, 1, CHUNK:], t1[HD:P], t2[HD:P], ALU.add))
                            nc.vector.tensor_copy(kd[HD:P, 0, CHUNK:], kd[0:HD, 0, CHUNK:])
                            nc.vector.tensor_copy(kd[0:HD, 1, CHUNK:], kd[HD:P, 1, CHUNK:]).then_inc(acc_dve, 1)
                            nc.vector.memset(vT[:, 0:CHUNK], 0.0).then_inc(v_pad, 1)
                    if i in (LT + 1, LT + 2):
                        for j in range(2 * (i - LT - 1), 2 * (i - LT - 1) + 2):
                            dve.wait_ge(aT_ready, l * LT + j + 1)
                            TT(I[:, j, :], I[:, j, :], xc[:, j, :], ALU.mult)
                            STT(out=R[:, j, :], in0=work[:, (j % 2) * SEQ:(j % 2 + 1) * SEQ], scalar=1.0,
                                in1=R[:, j, :], op0=ALU.add, op1=ALU.mult).then_inc(b2_ready, 1)
                    if i == LT + 4:
                        dve.wait_ge(root_ready, l + 1)
                        dve.wait_ge(b2_ready, (l + 1) * LT)
                        If = I[:, :, :].rearrange("p a b -> p (a b)")
                        link(TT(If, If, Rf, ALU.mult))
                    if i == LT + 5:
                        dve.wait_ge(vw_ready, l + 1)
                        for j in range(LT):
                            V.mark(nc.vector.tensor_tensor_scan(yt(AT + j), Adec[:, j, :], I[:, j, :], 0.0,
                                                                ALU.mult, ALU.add))
                    extra(i)
                    first_g = NPROJ - LT
                    if i >= first_g:
                        softmax(i - first_g)
                    if i == NPROJ - 1:
                        for t in range(QT):
                            out_squares(t)
                        dve.wait_ge(osq_ready, (l + 1) * QT)
                        dve.sem_inc(ssq_ready, 1)
                make_diag(norm_no(l, 0))
                dve.wait_ge(gelu_ready, l + 1)
                self_wait()
                for j in range(LT):
                    TT(yt(AT + j), yt(AT + j), xc[:, j, :], ALU.mult).then_inc(l_ready, 1)
                dve.wait_ge(lsq_ready, l * LT + 2)
                dve.wait_ge(cols_ready, norm_no(l, 0) + 1)
                link(TT(ssq[:, :], R[:, 0, :], R[:, 1, :], ALU.add))
                for j in range(2, LT):
                    dve.wait_ge(lsq_ready, l * LT + j + 1)
                    link(TT(ssq[:, :], ssq[:, :], R[:, j, :], ALU.add))
                dve.sem_inc(ssq_ready, 1)
                dve.wait_ge(rb_ready, norm_no(l, 0) + 1)
                make_diag(norm_no(l, 1))
                dve.wait_ge(rb_ready, norm_no(l, 1) + 1)
                split_src["f"] = yt
                split_tiles(conv_no(l, 0),
                            lambda j: pcol(l, "g_attn", j) if j < AT else pcol(l, "g_lru", j - AT),
                            lambda j: bank(2 if j < AT else 3), mL, None)
                for j in range(NOUT):
                    n = B + NPROJ + j
                    lo_chunk(n + 2, n % 2)
                    add_square(sq_no(l, 0), j)
                    extra(NPROJ + j)

                def add_to_x(which, k):
                    rb = bank(RB_BANK[k])
                    for j in range(KT):
                        link(STT(out=yt(j), in0=yt(j), scalar=fac[:, l, which, j:j + 1], in1=rb,
                                 op0=ALU.mult, op1=ALU.mult))
                        TT(xt(j), xt(j), yt(j), ALU.add).then_inc(x_done, 1)
                        if k == 2 or l + 1 < DEPTH:
                            if j > 0:
                                add_square(sq_no(l, 1 if k == 2 else 3), j - 1)
                    if k == 2 or l + 1 < DEPTH:
                        add_square(sq_no(l, 1 if k == 2 else 3), KT - 1)

                make_diag(norm_no(l, 2))
                factors(l, 1)
                dve.wait_ge(rb_ready, norm_no(l, 2) + 1)
                add_to_x(1, 2)
                factors(l, 2)
                make_diag(norm_no(l, 3))
                dve.wait_ge(rb_ready, norm_no(l, 3) + 1)
                split_src["f"] = xt
                split_tiles(conv_no(l, 1), lambda j: fac[:, l, 2, j:j + 1], lambda j: bank(RB_BANK[3]),
                            hL, mod[:, l * NMOD + 3, :])

                for g in range(GROUPS):
                    G = B + NPROJ + NOUT + g * GSTEP
                    U = l * 2 * PAIRS + g * 2 * KT
                    Q = l * PAIRS + g * KT
                    start, marks = V.n, V.marks
                    PER = 8
                    with dve.Fori(0, 2) as it:
                        V.n = it * PER + start
                        for c in range(8):
                            n = it * 8 + G + c
                            u = it * 8 + U + c
                            pr = it * 4 + Q + c // 2
                            lo_chunk(n + 2, c % 2)
                            dve.wait_ge(f_base, u + 1)
                            col = it * 4 + (g * KT + c // 2 + (c % 2) * PAIRS)
                            buf, acc = R[:, c % 4, :], bank(c % 4)
                            link(STT(out=buf[:, 1:], in0=acc[:, 0:SEQ - 1],
                                     scalar=par_l[:, bass.ds(col + (COLS["fcw"] + 2 * PAIRS), 1)],
                                     in1=buf[:, 1:], op0=ALU.mult, op1=ALU.add))
                            STT(out=buf[:, 2:], in0=acc[:, 0:SEQ - 2],
                                scalar=par_l[:, bass.ds(col + COLS["fcw"], 1)],
                                in1=buf[:, 2:], op0=ALU.mult, op1=ALU.add).then_inc(f_taps, 1)
                            if c % 2:
                                dve.wait_ge(f_taps, u + 1 + 4)
                                dve.wait_ge(f_gelu, pr + 1)
                                TT(I[:, 2 + (c // 2) % 2, :], I[:, (c // 2) % 2, :], buf, ALU.mult).then_inc(f_mul, 1)
                                dve.wait_ge(act_hi, pr + 1)
                                at = bass.ds(it * 4 + c // 2, 1)
                                TT(mL[:, at, :].rearrange("p a b -> p (a b)"), I[:, 2 + (c // 2) % 2, :],
                                   mH[:, at, :].rearrange("p a b -> p (a b)").bitcast(fp32),
                                   ALU.subtract).then_inc(act_lo, 1)
                            elif l == 0:
                                seg = it + (NMOD - 1 + 2 * g)
                                mac_unit(seg, c)
                                mac_unit(seg, c + 1)
                        if l == 0:
                            seg = it + (NMOD - 1 + 2 * g)
                            bl, bs = divmod(NMOD - 1 + 2 * g, NMOD)
                            if g == 0:
                                bcol = par[:, :, :].rearrange("p l c -> p (l c)")[
                                    :, bass.ds(it * (NPAR - (NMOD - 1) * KT) + (COLS["ada_b"] + (NMOD - 1) * KT), KT)]
                            else:
                                bcol = par[:, bl, :][:, bass.ds(it * KT + (COLS["ada_b"] + bs * KT), KT)]
                            mod_store(seg, l, bcol)
                    assert V.marks - marks == PER, V.marks - marks
                    V.n = start + 2 * PER
                    VD = G + 2 * KT
                    DN = l * GROUPS * KT + g * KT

                    def down(n, j, c, dn):
                        if not (isinstance(n, int) and n + 2 >= DEPTH * NCH):
                            lo_chunk(n + 2, c)
                        dve.wait_ge(chunk_done, n + 1)
                        acc = bank(4 + c)
                        out = yt(j) if isinstance(j, int) else y[:, :].rearrange("p (j q) -> p j q", j=KT)[
                            :, bass.ds(j, 1), :].rearrange("p a b -> p (a b)")
                        if g == 0:
                            nc.vector.tensor_copy(out, acc).then_inc(dn_read, 1)
                        else:
                            TT(out, acc, out, ALU.add).then_inc(dn_read, 1)

                    if g < GROUPS - 1:
                        with dve.Fori(0, KT // 2) as it:
                            for c in range(2):
                                down(it * 2 + (VD + c), it * 2 + c, c, None)
                    else:
                        for j in range(KT):
                            down(VD + j, j, j % 2, None)
                            if j:
                                add_square(sq_no(l, 2), j - 1)
                        add_square(sq_no(l, 2), KT - 1)
                make_diag(norm_no(l, 4))
                factors(l, 3)
                dve.wait_ge(rb_ready, norm_no(l, 4) + 1)
                add_to_x(3, 4)
                if l + 1 < DEPTH:
                    factors(l + 1, 0)
                    make_diag(norm_no(l, 5))
                    dve.wait_ge(rb_ready, norm_no(l, 5) + 1)
                    split_src["f"] = xt
                    split_tiles(conv_no(l, 2), lambda j: fac[:, l + 1, 0, j:j + 1],
                                lambda j: bank(RB_BANK[5]), hL, mod[:, (l + 1) * NMOD, :])

        @block.tensor
        def _(pe):
            def mm(out, a, b, start, stop, **kw):
                return nc.tensor.matmul(out, a, b, start=start, stop=stop, **kw)

            def tile_products(acc, slot, hi_, lo_, ready):
                for kt in range(KT):
                    if ready:
                        ready(kt)
                    a, al = wH[:, slot, kt * P:(kt + 1) * P], wL[:, slot, kt * P:(kt + 1) * P]
                    mm(acc, a, hi_[:, kt, :], kt == 0, False)
                    mm(acc, a, lo_[:, kt, :], False, False)
                    last = mm(acc, al, hi_[:, kt, :], False, kt == KT - 1)
                last.then_inc(chunk_done, 1)

            def norm_cols(m, mods):
                pe.wait_ge(ssq_ready, m + 1)
                if mods:
                    pe.wait_ge(mod_done, mods)
                for t in range(QT):
                    last = mm(bank(NORM_COLS)[:, t:t + 1], ssq[:, t * P:(t + 1) * P], ones[:, 0:1], True, True)
                last.then_inc(cols_ready, 1)

            def norm_spread(m, b):
                pe.wait_ge(diag_ready, m + 1)
                mm(bank(b), ones[:, :], diag, True, True).then_inc(rb_ready, 1)

            def mod_sum(seg, norms):
                pe.wait_ge(macc_ready, seg + 1)
                if norms:
                    pe.wait_ge(sd_ready, norms)
                if not (isinstance(seg, int) and seg == 0):
                    pe.wait_ge(mod_done, seg + 0)
                for j in range(KT):
                    last = mm(bank(NORM_COLS)[:, MODC + j:MODC + j + 1], macc[:, j * P:(j + 1) * P],
                              ones[:, 0:1], True, True)
                last.then_inc(mod_cols, 1)

            pe.wait_ge(consts, NCONST)
            mod_sum(0, 0)
            norm_cols(0, 0)
            mod_sum(1, 1)
            norm_spread(0, 2)

            for l in range(DEPTH):
                B = step_base(l)

                def gates(j):
                    rel, val = proj_release(l, j)
                    pe.wait_ge(rel, val)
                    if j >= 2:
                        pe.wait_ge(sig_done, l * LT + j - 1)
                    if j == 0:
                        pe.wait_ge(gw_in, 16 * (l + 1))
                    b = 2 + 2 * (j % 2)
                    mm(bank(b), gw[:, j, :], xc[:, j, :], True, True)
                    mm(bank(b + 1), gw[:, LT + j, :], xc[:, j, :], True, True).then_inc(gate_mm, 1)

                def values():
                    pe.wait_ge(acc_act, proj_release(l, LT + 1)[1])
                    pe.wait_ge(sig_done, (l + 1) * LT)
                    for w in range(SEQ // CHUNK):
                        last = nc.tensor.transpose(bank(4, 2)[:, w * P:(w + 1) * P],
                                                   vT[:, w * CHUNK:w * CHUNK + P], ident[:, :])
                    last.then_inc(vw_mm, 1)

                def scores_mm(t):
                    if t == 0:
                        rel, val = proj_release(l, NPROJ - LT - 1)
                        pe.wait_ge(rel, val)
                    else:
                        pe.wait_ge(s_copied, l * QT + t)
                    for s in range(NQ):
                        h = SLOTS[s]
                        at = HD * (h % 2)
                        for half in range(2):
                            w = (2 * t + half) * CHUNK
                            last = mm(bank(2, 2)[half * CHUNK:(half + 1) * CHUNK, s * P:(s + 1) * P],
                                      yt(h // 2)[at:at + HD, w:w + CHUNK],
                                      kd[at:at + HD, h // (NQ // NKV), w:w + P], True, True)
                    last.then_inc(s_mm, 1)

                def probs_transposed(t):
                    pe.wait_ge(p_ready, l * QT + t + 1)
                    if t == 0:
                        pe.wait_ge(vw_ready, l + 1)
                    else:
                        pe.wait_ge(pt_copied, l * QT + t)
                    for s in range(NQ):
                        last = nc.tensor.transpose(bank(4, 2)[:, s * P:(s + 1) * P],
                                                   scores[t % 2][:, s * P:(s + 1) * P], ident[:, :])
                    last.then_inc(pt_mm, 1)

                def outputs_mm(t):
                    pe.wait_ge(pt_copied, l * QT + t + 1)
                    if t:
                        pe.wait_ge(o_copied, l * QT + t)
                    pt = probsT[t % 2].rearrange("p (s q) -> p s q", s=NQ)
                    o4 = bank(6).rearrange("p (j q) -> p j q", j=AT)
                    for kv in range(NKV):
                        for half in range(2):
                            for odd in range(2):
                                last = mm(o4[HD * odd:HD * (odd + 1), 2 * kv:2 * kv + 2,
                                             half * CHUNK:(half + 1) * CHUNK],
                                          vw[:, 2 * t + half, kv * HD:(kv + 1) * HD],
                                          pt[:, 4 * odd + 2 * kv:4 * odd + 2 * kv + 2,
                                             half * CHUNK:(half + 1) * CHUNK], True, True)
                    last.then_inc(o_mm, 1)

                for i, kind in enumerate(PROJ):
                    n = B + i
                    pe.wait_ge(w_lo, n + 1)
                    if i >= 2:
                        pe.wait_ge(*proj_release(l, i - 2))
                    k0 = 0 if l == 0 else conv_no(l - 1, 2)
                    ready = (lambda kt: pe.wait_ge(lo_ready, k0 + kt + 1)) if i == 0 else None
                    tile_products(bank(i % 2), n % 2, hH, hL, ready)
                    if 1 <= i <= LT:
                        gates(i - 1)
                    if i == LT + 3:
                        values()
                    first_g = NPROJ - LT
                    if i == first_g:
                        scores_mm(0)
                    if i == first_g + 1:
                        scores_mm(1)
                    if i == first_g + 2:
                        probs_transposed(0)
                        scores_mm(2)
                    if i == first_g + 3:
                        outputs_mm(0)
                        probs_transposed(1)
                        scores_mm(3)
                        outputs_mm(1)
                        probs_transposed(2)
                        outputs_mm(2)
                        probs_transposed(3)
                        outputs_mm(3)
                    if i in MOD_AT[l]:
                        mod_sum(MOD_AT[l][i], norm_no(l, 0))
                mods = 3 if l == 0 else 11
                norm_cols(norm_no(l, 0), mods)
                norm_spread(norm_no(l, 0), RB_BANK[0])
                pe.wait_ge(sd_ready, norm_no(l, 0) + 1)
                norm_cols(norm_no(l, 1), mods)
                norm_spread(norm_no(l, 1), RB_BANK[1])
                for j in range(NOUT):
                    n = B + NPROJ + j
                    pe.wait_ge(w_lo, n + 1)
                    if j < 2:
                        pe.wait_ge(*proj_release(l, NPROJ - 2 + j))
                    else:
                        pe.wait_ge(sq_ready, sq_no(l, 0) + j - 1)
                    ready = (lambda kt: pe.wait_ge(lo_ready, conv_no(l, 0) + kt + 1)) if j == 0 else None
                    tile_products(bank(j % 2), n % 2, mH, mL, ready)
                    if NPROJ + j in MOD_AT[l]:
                        mod_sum(MOD_AT[l][NPROJ + j], norm_no(l, 2))
                mods = 5 if l == 0 else 12
                norm_cols(norm_no(l, 2), mods)
                norm_spread(norm_no(l, 2), RB_BANK[2])
                norm_cols(norm_no(l, 3), mods)
                norm_spread(norm_no(l, 3), RB_BANK[3])
                for g in range(GROUPS):
                    G = B + NPROJ + NOUT + g * GSTEP
                    U = l * 2 * PAIRS + g * 2 * KT
                    with pe.Fori(0, 2) as it:
                        for c in range(8):
                            pe.wait_ge(w_lo, it * 8 + (G + c + 1))
                            pe.wait_ge(f_taps, it * 8 + (U + c + 1))
                            ready = (lambda kt: pe.wait_ge(lo_ready, conv_no(l, 1) + kt + 1)) if c == 0 else None
                            tile_products(bank(c % 4), c % 2, hH, hL, ready)
                        if l == 0:
                            mod_sum(it + (NMOD - 1 + 2 * g), norm_no(l, 4))
                    DN = l * GROUPS * KT + g * KT
                    VD = G + 2 * KT
                    with pe.Fori(0, KT // 2) as it:
                        for c in range(2):
                            pe.wait_ge(w_lo, it * 2 + (VD + c + 1))
                            pe.wait_ge(dn_read, it * 2 + (DN + c + 1))
                            ready = (lambda kt: pe.wait_ge(act_lo, l * PAIRS + g * KT + kt + 1)) if c == 0 else None
                            tile_products(bank(4 + c), c, mH, mL, ready)
                mods = 11 if l == 0 else 12
                norm_cols(norm_no(l, 4), mods)
                norm_spread(norm_no(l, 4), RB_BANK[4])
                if l + 1 < DEPTH:
                    norm_cols(norm_no(l, 5), mods)
                    norm_spread(norm_no(l, 5), RB_BANK[5])


def columns(a):
    a = np.asarray(a)
    return np.swapaxes(a.reshape(*a.shape[:-1], a.shape[-1] // P, P), -1, -2)


def kernel(**inputs):
    import concourse.bacc as bacc
    from concourse.bass_utils import run_bass_kernel_spmd

    a = {k: np.asarray(v) for k, v in inputs.items()}
    L = DEPTH

    def tiles(w, n_k):
        w = w.reshape(n_k, P, w.shape[1] // P, P)
        return w.transpose(2, 1, 0, 3)
    stream = np.empty((L, NCH, P, KT, P), np.float32)
    kv = NKV * HD
    starts = {"q": 0, "k": D_ATTN, "v": D_ATTN + kv, "x": D_ATTN + 2 * kv, "g": D_ATTN + 2 * kv + D_LRU}
    for l in range(L):
        w_in = tiles(a["w_in"][l], KT)
        seen = dict.fromkeys(starts, 0)
        for i, kind in enumerate(PROJ):
            stream[l, i] = w_in[starts[kind] // P + seen[kind]]
            seen[kind] += 1
        stream[l, NPROJ:NPROJ + NOUT] = tiles(a["w_out"][l], KT)
        up = tiles(a["ffn_w_up"][l], KT)
        down = tiles(a["ffn_w_down"][l], PAIRS)
        at = NPROJ + NOUT
        for g in range(GROUPS):
            for i in range(KT):
                stream[l, at] = up[g * KT + i]
                stream[l, at + 1] = up[PAIRS + g * KT + i]
                at += 2
            stream[l, at:at + KT] = down[:, :, g * KT:(g + 1) * KT, :]
            at += KT
    stream = stream.reshape(L * NCH, P, KT * P)

    ada = a["ada_w"].reshape(L, KT, P, NMOD, D).transpose(0, 3, 1, 2, 4)
    ada = np.ascontiguousarray(ada).reshape(L * NMOD * KT, P, D)

    gw = np.zeros((L, P, 2 * LT, P), np.float32)
    for which, name in enumerate(("lru_w_a", "lru_w_x")):
        w = a[name]
        for j in range(LT):
            for b in range(2):
                s = slice(b * 64, b * 64 + 64)
                gw[:, s, which * LT + j, s] = w[:, 2 * j + b]

    par = np.empty((L, P, NPAR), np.float32)

    def put(name, cols):
        par[:, :, COLS[name]:COLS[name] + cols.shape[-1]] = cols
    for name, key in [("mix_pre", "mix_pre_g"), ("mix_post", "mix_post_g"), ("ffn_pre", "ffn_pre_g"),
                      ("ffn_post", "ffn_post_g"), ("g_attn", "grp_g_attn"), ("g_lru", "grp_g_lru"),
                      ("lcb", "lru_conv_b"), ("ba", "lru_b_a"), ("bx", "lru_b_x"), ("lam", "lru_lambda"),
                      ("fcb", "ffn_conv_b"), ("ada_b", "ada_b")]:
        put(name, columns(a[key]))
    put("lcw", columns(a["lru_conv_w"].reshape(L, CONVW * D_LRU)))
    put("fcw", columns(a["ffn_conv_w"].reshape(L, FCONV * 2 * DFF)))
    put("sink", np.broadcast_to(a["attn_sinks"][:, None, SLOTS], (L, P, NQ)))

    half = HD // 2
    inv = (THETA ** (-np.arange(0, HD, 2, dtype=np.float64) / HD)).astype(np.float32)
    arrays = {
        "in_w": stream, "in_ada": ada, "in_gw": gw, "in_par": par,
        "in_x": np.ascontiguousarray(a["x"][0].reshape(SEQ, KT, P).transpose(2, 1, 0)).reshape(P, KT * SEQ),
        "in_c": np.ascontiguousarray(columns(a["c"][0])),
        "in_pos": np.ascontiguousarray(np.broadcast_to(a["positions"][0][None, :], (P, SEQ))),
        "in_inv_freq": np.tile(inv, P // half).reshape(P, 1),
    }
    nc = bacc.Bacc("TRN2", target_bir_lowering=False, num_devices=1)
    A = {}
    for name, arr in arrays.items():
        A[name[3:]] = nc.dram_tensor(name, arr.shape, mybir.dt.from_np(arr.dtype), kind="ExternalInput").ap()
    A["out"] = nc.dram_tensor("out_0", (P, KT * SEQ), mybir.dt.float32, kind="ExternalOutput").ap()
    build(nc, A)
    r = run_bass_kernel_spmd(nc, [arrays], core_ids=[0])
    out = r.results[0]["out_0"]
    return np.ascontiguousarray(out.reshape(P, KT, SEQ).transpose(2, 1, 0)).reshape(1, SEQ, D)
```

```python
import numpy as np
import concourse.bass as bass
from concourse import mybir
from contextlib import ExitStack

P = 128
DEPTH, SEQ, D = 2, 512, 1024
CHUNK, HD, NQ, NKV = 64, 64, 8, 2
D_ATTN, D_LRU = 512, 512
DFF = 3072
EPS = 1e-6
MASK = -1e30
THETA = 10000.0
KT = D // P
AT, LT = D_ATTN // P, D_LRU // P
QT = SEQ // P
PAIRS = DFF // P
GROUPS = PAIRS // KT
PROJ = ["x"] * LT + ["k"] + ["q"] * AT + ["v"] + ["g"] * LT
NPROJ = len(PROJ)
NOUT = KT
GSTEP = 3 * KT
NCH = NPROJ + NOUT + GROUPS * GSTEP
NMOD = 6
CONVW = 4
FCONV = 3
SLOTS = [2 * (s % 4) + s // 4 for s in range(NQ)]

COLS = {}
_at = 0
for _name, _n in [("mix_pre", KT), ("mix_post", KT), ("ffn_pre", KT), ("ffn_post", KT),
                  ("g_attn", AT), ("g_lru", LT), ("lcw", CONVW * LT), ("lcb", LT), ("ba", LT),
                  ("bx", LT), ("lam", LT), ("fcw", FCONV * 2 * PAIRS), ("fcb", 2 * PAIRS),
                  ("ada_b", NMOD * KT), ("sink", NQ)]:
    COLS[_name] = _at
    _at += _n
NPAR = _at

TWO_PI = 6.283185307179586
def _parts(value, bits, n):
    out = []
    for i in range(n):
        if i == n - 1:
            out.append(float(np.float32(value)))
        else:
            q = 2.0 ** (np.floor(np.log2(value)) - bits + 1)
            part = float(np.floor(value / q) * q)
            out.append(part)
            value -= part
    return out
PI_PARTS = _parts(TWO_PI, 11, 3)
ROUND_MAGIC = float(1.5 * 2 ** 23)
COARSE = 1024.0


class Tally:

    def __init__(self, sem):
        self.sem, self.n, self.marks = sem, 0, 0

    def mark(self, instruction):
        instruction.then_inc(self.sem, 1)
        self.n = self.n + 1
        self.marks += 1


def build(nc, A):
    fp32, fp32r, i32 = mybir.dt.float32, mybir.dt.float32r, mybir.dt.int32
    ALU, ACT, AX = mybir.AluOpType, mybir.ActivationFunctionType, mybir.AxisListType
    ctx = ExitStack()
    with ctx:
        def sb(name, shape, dt=fp32):
            return ctx.enter_context(nc.sbuf_tensor("sb_" + name, shape, dt))

        def sem(name):
            return ctx.enter_context(nc.semaphore(name))

        x = sb("x", [P, KT * SEQ])
        hH = sb("hH", [P, KT, SEQ], fp32r)
        hL = sb("hL", [P, KT, SEQ], fp32r)
        mH = sb("mH", [P, KT, SEQ], fp32r)
        mL = sb("mL", [P, KT, SEQ], fp32r)
        y = sb("y", [P, KT * SEQ])
        raw = sb("raw", [P, 2, KT * P])
        wH = sb("wH", [P, 2, KT * P], fp32r)
        wL = sb("wL", [P, 2, KT * P], fp32r)
        adaw = sb("adaw", [P, 4, D])
        macc = sb("macc", [P, D])
        par = sb("par", [P, DEPTH, NPAR])
        mod = sb("mod", [P, DEPTH * NMOD, KT])
        fac = sb("fac", [P, DEPTH, 4, KT])
        gw = sb("gw", [P, 2 * LT, P])
        ones = sb("ones", [P, P])
        ident = sb("ident", [P, P])
        R = sb("R", [P, 4, SEQ])
        I = sb("I", [P, 4, SEQ])
        Adec = sb("Adec", [P, 4, SEQ])
        xc = sb("xc", [P, 4, SEQ])
        kd = sb("kd", [P, NKV, CHUNK + SEQ])
        vw = sb("vw", [P, 8, P])
        scr = sb("scr", [P, 2 * SEQ])
        work = sb("work", [P, 2 * SEQ])
        cosT = sb("cosT", [P, SEQ])
        sinT = sb("sinT", [P, SEQ])
        sq = sb("sq", [P, SEQ])
        ssqv = sb("ssqv", [P, CHUNK + SEQ])
        ssq = ssqv[:, 0:SEQ]
        msum = sb("msum", [P, KT])
        tiny = sb("tiny", [P, 96])

        ps = ctx.enter_context(nc.psum_tensor("ps", [P, 8 * SEQ], fp32))

        def bank(b, n=1):
            return ps[:, b * SEQ:(b + n) * SEQ]

        def xt(j):
            return x[:, j * SEQ:(j + 1) * SEQ]

        def yt(j):
            return y[:, j * SEQ:(j + 1) * SEQ]

        vT = ssqv[:, :]
        Rf = R[:, :, :].rearrange("p a b -> p (a b)")
        scores = [work[:, :], Rf[:, 0:2 * SEQ]]
        probsT = [scr[:, :], Rf[:, 2 * SEQ:4 * SEQ]]
        sqb = [sq[:, :], work[:, SEQ:2 * SEQ]]
        xsqb = [sq[:, :], work[:, SEQ:2 * SEQ], work[:, 0:SEQ], ssq]
        NORM_COLS = 7

        def pcol(l, name, i=0):
            c = COLS[name] + i
            return par[:, l, c:c + 1]

        mx = [tiny[:, 0:8], tiny[:, 8:16]]
        den = [tiny[:, 16:24], tiny[:, 24:32]]
        es = [tiny[:, 32:40], tiny[:, 40:48]]
        eps = tiny[:, 56:57]
        sign = tiny[:, 57:58]
        freq = tiny[:, 58:59]
        sd8 = tiny[:, 48:56]
        rs8 = tiny[:, 88:96]
        csil = tiny[:, 64:72]
        craw = tiny[:, 72:80]
        ctmp = tiny[:, 80:88]
        spl = sb("spl", [P, DEPTH, LT])
        nspl = sb("nspl", [P, DEPTH, LT])
        sp1 = sb("sp1", [P, DEPTH, LT])
        sp2 = sb("sp2", [P, DEPTH, LT])
        sp3 = sb("sp3", [P, DEPTH, LT])

        w_in = [sem("w_in0"), sem("w_in1")]
        w_hi, w_lo = sem("w_hi"), sem("w_lo")
        chunk_done = sem("chunk_done")
        ada_in = [sem(f"ada_in{i}") for i in range(4)]
        ada_used = sem("ada_used")
        macc_ready, mod_cols, mod_done = sem("macc_ready"), sem("mod_cols"), sem("mod_done")
        early_in, params_in, gw_in = sem("early_in"), sem("params_in"), sem("gw_in")
        x_in = [sem("x_in0"), sem("x_in1")]
        consts = sem("consts")
        dve_self, act_self = sem("dve_self"), sem("act_self")
        c_exp, sp_exp, sp_recip, sp_ready = sem("c_exp"), sem("sp_exp"), sem("sp_recip"), sem("sp_ready")
        presq_ready, presq_used, pool_self = sem("presq_ready"), sem("presq_used"), sem("pool_self")
        ang_ready, sin_ready, rope_ready = sem("ang_ready"), sem("sin_ready"), sem("rope_ready")
        ssq_ready, cols_ready, sd_ready = sem("ssq_ready"), sem("cols_ready"), sem("sd_ready")
        rs_ready, rb_ready = sem("rs_ready"), sem("rb_ready")
        xsq_ready, xsq_used, sd_row, sd_cols = sem("xsq_ready"), sem("xsq_used"), sem("sd_row"), sem("sd_cols")
        xsum_ready, x_done2 = sem("xsum_ready"), sem("x_done2")
        sq_ready, sq_used = sem("sq_ready"), sem("sq_used")
        tmp_ready, hi_ready, lo_ready = sem("tmp_ready"), sem("hi_ready"), sem("lo_ready")
        x_done, y_scaled = sem("x_done"), sem("y_scaled")
        den_ready, scan_done, pt_last = sem("den_ready"), sem("scan_done"), sem("pt_last")
        p_last = sem("p_last")
        x_base, acc_dve, acc_act = sem("x_base"), sem("acc_dve"), sem("acc_act")
        swap_ready, v_pad = sem("swap_ready"), sem("v_pad")
        gate_mm, sig_done, aT_ready, b2_ready = sem("gate_mm"), sem("sig_done"), sem("aT_ready"), sem("b2_ready")
        root_ready = sem("root_ready")
        vw_mm, vw_ready = sem("vw_mm"), sem("vw_ready")
        s_mm, s_copied, s_sub, s_exp, p_ready = sem("s_mm"), sem("s_copied"), sem("s_sub"), sem("s_exp"), sem("p_ready")
        pt_mm, pt_copied, o_mm, o_copied, osq_ready = sem("pt_mm"), sem("pt_copied"), sem("o_mm"), sem("o_copied"), sem("osq_ready")
        gelu_ready, l_ready, lsq_ready = sem("gelu_ready"), sem("l_ready"), sem("lsq_ready")
        out_copied = sem("out_copied")
        f_base, f_taps, f_gelu, f_mul = sem("f_base"), sem("f_taps"), sem("f_gelu"), sem("f_mul")
        act_hi, act_lo, dn_read = sem("act_hi"), sem("act_lo"), sem("dn_read")
        stored = sem("stored")
        block = ctx.enter_context(nc.Block())

        NORMS = 5
        def norm_no(l, k):
            return 1 + l * NORMS + k
        X_NORMS = [norm_no(0, 2), norm_no(0, 4), norm_no(1, 2)]
        COL_NORMS = [m for m in range(norm_no(1, 3) + 1) if m not in X_NORMS]
        SPARE = 3
        XSUM = 0
        X_DVE = [2, 5, 7]
        X_POOL = [j for j in range(KT) if j not in X_DVE]
        def x_new(l, k, j):
            mine, s_ = (X_DVE, x_done2) if j in X_DVE else (X_POOL, x_done)
            return s_, (2 * l + k) * len(mine) + mine.index(j) + 1
        RB_BANK = [2, 4, 5, 6, 2]
        def conv_no(l, k):
            return KT + l * 3 * KT + k * KT
        presq = [work[:, 0:SEQ], work[:, SEQ:2 * SEQ], sq[:, :]]
        def sq_no(l, k):
            return l * 2 * KT + k * KT

        def proj_release(l, i):
            dve_kinds = "xkq"
            if PROJ[i] in dve_kinds:
                per = sum(k in dve_kinds for k in PROJ)
                return acc_dve, l * per + sum(k in dve_kinds for k in PROJ[:i + 1])
            per = sum(k not in dve_kinds for k in PROJ)
            return acc_act, l * per + sum(k not in dve_kinds for k in PROJ[:i + 1])

        MAC_STEPS = {0: {0: [0], 1: [1], 2: [2], 3: [3], 4: [4], 5: [5], 6: [6, 7],
                         9: [8, 9],
                         13: [10, 11, 12], 14: [13, 14, 15], 16: [16, 17], 17: [18, 19], 18: [20, 21],
                         19: [22, 23]},
                     1: {14 + i: [i] for i in range(4)} | {18: [4, 5], 19: [6, 7]}}
        MAC_FIRST = {0: 2 * KT, 1: 11 * KT}
        MOD_AT = {0: {8: 2, 15: 3, 20: 4}, 1: {20: 11}}
        UP_MACS = {0: [0, 1], 1: [2], 2: [3, 4], 3: [5], 4: [6], 5: [7]}

        def step_base(l):
            return l * NCH

        @block.sync
        def _(sp):
            sp.dma_start(craw, A["c"]).then_inc(early_in, 16)
            sp.dma_start(freq, A["inv_freq"]).then_inc(early_in, 16)
            sp.dma_start(Adec[:, 0, :].bitcast(i32), A["pos"]).then_inc(early_in, 16)
            sp.dma_start(par[:, :, :], A["par"].rearrange("l p c -> p l c")).then_inc(params_in, 16)
            half = KT * SEQ // 2
            for h in range(2):
                sp.dma_start(x[:, h * half:(h + 1) * half], A["x"][:, h * half:(h + 1) * half]).then_inc(x_in[h], 16)
            stream = A["w"]
            for s in range(4):
                sp.dma_start(adaw[:, s, :], A["ada"][s]).then_inc(ada_in[s], 16)

            def refill(n, parity):
                sp.wait_ge(w_lo, n - 1)
                src = stream[n] if isinstance(n, int) else stream[bass.ds(n, 1)].rearrange("a p c -> p (a c)")
                sp.dma_start(raw[:, parity, :], src).then_inc(w_in[parity], 16)

            def ada_refill(u, slot):
                sp.wait_ge(ada_used, u - 3)
                src = A["ada"][u] if isinstance(u, int) else A["ada"][bass.ds(u, 1)].rearrange("a p c -> p (a c)")
                sp.dma_start(adaw[:, slot, :], src).then_inc(ada_in[slot], 16)

            for u in range(4, 2 * KT):
                if u == 2 * KT - 2:
                    for s in range(2):
                        sp.dma_start(raw[:, s, :], stream[s]).then_inc(w_in[s], 16)
                ada_refill(u, u % 4)
            for n in (2, 3):
                refill(n, n % 2)
            for u in range(2 * KT, 2 * KT + 4):
                ada_refill(u, u % 4)
            sp.dma_start(gw[:, :, :], A["gw"][0]).then_inc(gw_in, 16)
            for l in range(DEPTH):
                B = step_base(l)
                for i in range(NPROJ + NOUT):
                    refill(B + i + 4, i % 2)
                    for k in MAC_STEPS[l].get(i, []):
                        u = MAC_FIRST[l] + k + 4
                        if u < DEPTH * NMOD * KT:
                            ada_refill(u, u % 4)
                for g in range(GROUPS):
                    G = B + NPROJ + NOUT + g * GSTEP
                    with sp.Fori(0, 2) as it:
                        for c in range(8):
                            refill(it * 8 + (G + c + 4), c % 2)
                            if l == 0:
                                for kt in UP_MACS.get(c, []):
                                    ada_refill(it * KT + ((NMOD - 1 + 2 * g) * KT + kt + 4), kt % 4)
                    if l + 1 < DEPTH or g + 1 < GROUPS:
                        with sp.Fori(0, KT // 2) as it:
                            for c in range(2):
                                refill(it * 2 + (G + 2 * KT + c + 4), c)
                    else:
                        for j in range(KT - 4):
                            refill(G + 2 * KT + j + 4, j % 2)
            for j in range(KT):
                sp.wait_ge(*x_new(DEPTH - 1, 1, j))
                sp.dma_start(A["out"][:, j * SEQ:(j + 1) * SEQ], xt(j)).then_inc(stored, 16)
            sp.wait_ge(stored, 16 * KT)

        @block.gpsimd
        def _(pool):
            made = 0

            def const(tile, value):
                nonlocal made
                nc.gpsimd.memset(tile, value).then_inc(consts, 1)
                made += 1
                pool.wait_ge(consts, made)
            const(ident[:, :], 0.0)
            const(ones[:, :], 1.0)
            const(eps, EPS)
            const(kd[:, :, 0:CHUNK], 0.0)
            for q4 in range(4):
                const(sign[32 * q4:32 * q4 + 32, :], -1.0 if q4 % 2 == 0 else 1.0)
            nc.gpsimd.affine_select(out=ident[:, :], in_=ident[:, :], compare_op=ALU.not_equal, fill=1.0,
                                    base=0, pattern=[[-1, P]], channel_multiplier=1).then_inc(consts, 1)
            GTT, GTS = nc.gpsimd.tensor_tensor, nc.gpsimd.tensor_scalar
            W = Tally(pool_self)

            def link(ins):
                W.mark(ins)
                pool.wait_ge(pool_self, W.n)

            pool.wait_ge(presq_ready, 1)
            for j in range(1, KT):
                pool.wait_ge(presq_ready, j + 1)
                GTT(ssq, ssq, presq[(j - 1) % 3], ALU.add).then_inc(presq_used, 1)
                pool.wait_ge(presq_used, j)
            pool.wait_ge(sin_ready, 2)
            link(GTS(sinT[:, :], sinT[:, :], sign, 0.0, ALU.mult, ALU.add))
            link(GTT(cosT[:, :], cosT[:, :], cosT[:, :], ALU.mult))
            GTS(cosT[:, :], cosT[:, :], -2.0, 1.0, ALU.mult, ALU.add).then_inc(rope_ready, 1)
            pool.wait_ge(sp_recip, 1)
            lam = par[:, :, COLS["lam"]:COLS["lam"] + LT]
            s1, s2, s3 = sp1[:, :, :], sp2[:, :, :], sp3[:, :, :]
            link(GTT(s2, s2, s1, ALU.mult))
            link(GTT(s1, s2, s2, ALU.mult))
            link(GTS(s3, s1, 1.0 / 17, 1.0 / 15, ALU.mult, ALU.add))
            for k in range(13, 0, -2):
                link(GTT(s3, s3, s1, ALU.mult))
                link(GTS(s3, s3, 1.0 / k, 1.0, ALU.add, ALU.mult))
            link(GTT(s3, s3, s2, ALU.mult))
            link(GTS(s1, lam, -0.5, 0.0, ALU.mult, ALU.max))
            link(GTT(s3, s3, s1, ALU.add))
            link(GTS(spl[:, :, :], s3, 8.0, 0.0, ALU.mult, ALU.add))
            GTS(nspl[:, :, :], s3, -16.0, 0.0, ALU.mult, ALU.add).then_inc(sp_ready, 1)

            def add_to_x(l, k):
                for j in X_POOL:
                    pool.wait_ge(y_scaled, (2 * l + k) * KT + j + 1)
                    GTT(xt(j), xt(j), yt(j), ALU.add).then_inc(x_done, 1)

            for l in range(DEPTH):
                for t in range(QT - 1):
                    pool.wait_ge(den_ready, l * (QT - 1) + t + 1)
                    sc = scores[t % 2].rearrange("p (s k) -> p s k", s=NQ)
                    GTT(sc, sc, den[t % 2].unsqueeze(2).broadcast_to([P, NQ, P]), ALU.mult).then_inc(p_ready, 1)
                pool.wait_ge(scan_done, (l + 1) * LT)
                pool.wait_ge(gelu_ready, l + 1)
                for j in range(LT):
                    GTT(yt(AT + j), yt(AT + j), xc[:, j, :], ALU.mult).then_inc(l_ready, 1)
                add_to_x(l, 0)
                add_to_x(l, 1)
        NCONST = 9

        @block.scalar
        def _(act):
            S = Tally(act_self)

            def self_wait():
                act.wait_ge(act_self, S.n)

            def hi(n, first=False):
                s = n_par(n)
                if not first:
                    act.wait_ge(chunk_done, n - 1)
                act.wait_ge(w_in[s], w_count(n))
                nc.scalar.activation(wH[:, s, :], raw[:, s, :], ACT.Copy).then_inc(w_hi, 1)

            state = {"par": 0}

            def n_par(n):
                return state["par"]

            def w_count(n):
                return state["wc"]

            def split_step(n, parity, first=False):
                state["par"] = parity
                state["wc"] = (n - parity) * 8 + 16
                hi(n, first)

            def fetch_sqrt():
                nc.scalar.activation(tiny[:, 60:61], eps, ACT.Sqrt)

            def sd_step(m, dim, groups=1):
                act.wait_ge(cols_ready, COL_NORMS.index(m) + 1)
                nc.scalar.activation(sd8[:, 0:groups * QT], bank(NORM_COLS)[:, 0:groups * QT], ACT.Sqrt, bias=eps,
                                     scale=1.0 / dim).then_inc(sd_ready, 1)

            def squares_of(m0, j, src, wait_sem, wait_value, own=False):
                if not own:
                    act.wait_ge(wait_sem, wait_value)
                if j >= 2:
                    act.wait_ge(sq_used, m0 + j - 1)
                dst = ssq if j == 0 else sqb[j % 2]
                nc.scalar.activation(dst, src, ACT.Square).then_inc(sq_ready, 1)

            def x_norm(l, k):
                i = X_NORMS.index(norm_no(l, k + 1))
                for j in range(KT):
                    act.wait_ge(*x_new(l, k // 2, j))
                    if j >= 4:
                        act.wait_ge(xsq_used, i * (KT - 1) + j - 3)
                    nc.scalar.activation(xsqb[j % 4], xt(j), ACT.Square).then_inc(xsq_ready, 1)
                act.wait_ge(xsum_ready, i + 1)
                nc.scalar.activation(ssq[0:1, :], bank(XSUM)[0:1, :], ACT.Sqrt, bias=eps[0:1, :],
                                     scale=1.0 / D).then_inc(sd_row, 1)

            def hi_tiles(k0, dst, bias):
                for j in range(KT):
                    act.wait_ge(tmp_ready, k0 + j + 1)
                    if bias is None:
                        nc.scalar.activation(dst[:, j, :], yt(j), ACT.Copy).then_inc(hi_ready, 1)
                    else:
                        nc.scalar.activation(dst[:, j, :], yt(j), ACT.Identity,
                                             bias=bias[:, j:j + 1], scale=1.0).then_inc(hi_ready, 1)

            act.wait_ge(early_in, 48)
            nc.scalar.activation(ctmp, craw, ACT.Exp, scale=-1.0).then_inc(c_exp, 1)
            act.wait_ge(params_in, 16)
            lam = par[:, :, COLS["lam"]:COLS["lam"] + LT]
            S.mark(nc.scalar.activation(sp1[:, :, :], lam, ACT.Abs))
            self_wait()
            nc.scalar.activation(sp2[:, :, :], sp1[:, :, :], ACT.Exp, scale=-1.0).then_inc(sp_exp, 1)
            for j in range(KT):
                if j % (KT // 2) == 0:
                    act.wait_ge(x_in[j // (KT // 2)], 16)
                if j >= 4:
                    act.wait_ge(presq_used, j - 3)
                nc.scalar.activation(presq[(j - 1) % 3] if j else ssq, xt(j), ACT.Square).then_inc(presq_ready, 1)
                if j == 2:
                    act.wait_ge(ang_ready, 1)
                    nc.scalar.activation(sinT[:, :], R[:, 0, :], ACT.Sin).then_inc(sin_ready, 1)
                    nc.scalar.activation(cosT[:, :], R[:, 0, :], ACT.Sin, scale=0.5).then_inc(sin_ready, 1)
            sd_step(0, D)
            split_step(0, 0, True)
            split_step(1, 1, True)
            act.wait_ge(mod_done, 2)
            hi_tiles(0, hH, mod[:, 0, :])

            for l in range(DEPTH):
                B = step_base(l)
                par_l = par[:, l, :]
                for i, kind in enumerate(PROJ):
                    n = B + i
                    split_step(n + 2, n % 2)
                    acc = bank(i % 2)
                    first_g = NPROJ - LT
                    act.wait_ge(chunk_done, n + 1)
                    if kind == "x":
                        nc.scalar.activation(xc[:, i, :], acc, ACT.Identity, bias=pcol(l, "lcb", i),
                                             scale=pcol(l, "lcw", (CONVW - 1) * LT + i)).then_inc(x_base, 1)
                    elif kind in "kq":
                        if kind == "q":
                            act.wait_ge(*proj_release(l, i - 1))
                        for q4 in range(4):
                            o = q4 ^ 1
                            last = nc.scalar.activation(scr[32 * q4:32 * q4 + 32, 0:SEQ],
                                                        acc[32 * o:32 * o + 32, :], ACT.Copy)
                        last.then_inc(swap_ready, 1)
                    elif kind == "v":
                        act.wait_ge(v_pad, l + 1)
                        nc.scalar.activation(vT[:, CHUNK:], acc, ACT.Copy).then_inc(acc_act, 1)
                    else:
                        j = i - (NPROJ - LT)
                        if j == 0:
                            act.wait_ge(b2_ready, (l + 1) * LT)
                        nc.scalar.activation(xc[:, j, :], acc, ACT.Copy).then_inc(acc_act, 1)
                    if 1 <= i <= LT:
                        j = i - 1
                        act.wait_ge(gate_mm, l * LT + j + 1)
                        b = 2 + 2 * (j % 2)
                        S.mark(nc.scalar.activation(R[:, j, :], bank(b), ACT.Sigmoid, bias=pcol(l, "ba", j)))
                        nc.scalar.activation(I[:, j, :], bank(b + 1), ACT.Sigmoid,
                                             bias=pcol(l, "bx", j)).then_inc(sig_done, 1)
                    if l == 0 and i == LT + 1:
                        act.wait_ge(sp_ready, 1)
                    if i in (LT + 1, LT + 2):
                        for j in range(2 * (i - LT - 1), 2 * (i - LT - 1) + 2):
                            self_wait()
                            S.mark(nc.scalar.activation(Adec[:, j, :], R[:, j, :], ACT.Exp,
                                                        scale=nspl[:, l, j:j + 1]))
                            self_wait()
                            nc.scalar.activation(R[:, j, :], R[:, j, :], ACT.Tanh,
                                                 scale=spl[:, l, j:j + 1]).then_inc(aT_ready, 1)
                    if i == LT + 3:
                        act.wait_ge(b2_ready, (l + 1) * LT)
                        nc.scalar.activation(Rf, Rf, ACT.Sqrt).then_inc(root_ready, 1)
                    if i == first_g + 1:
                        act.wait_ge(vw_mm, l + 1)
                        nc.scalar.activation(vw[:, :, :].rearrange("p a b -> p (a b)"), bank(4, 2),
                                             ACT.Copy).then_inc(vw_ready, 1)

                    def copy_scores(t):
                        act.wait_ge(s_mm, l * QT + t + 1)
                        if t >= 2:
                            act.wait_ge(pt_mm, l * QT + t - 1)
                        nc.scalar.activation(scores[t % 2], bank(2, 2), ACT.Copy,
                                             scale=HD ** -0.5).then_inc(s_copied, 1)

                    def exps(t):
                        act.wait_ge(s_sub, l * QT + t + 1)
                        nc.scalar.activation(es[t % 2], es[t % 2], ACT.Exp)
                        nc.scalar.activation(scores[t % 2], scores[t % 2], ACT.Exp).then_inc(s_exp, 1)

                    def copy_pt(t):
                        act.wait_ge(pt_mm, l * QT + t + 1)
                        if t >= 2:
                            act.wait_ge(o_mm, l * QT + t - 1)
                        nc.scalar.activation(probsT[t % 2], bank(4, 2), ACT.Copy).then_inc(pt_copied, 1)

                    def copy_out(t):
                        act.wait_ge(o_mm, l * QT + t + 1)
                        o4 = bank(6).rearrange("p (j q) -> p j q", j=AT)
                        dst = y[:, 0:AT * SEQ].rearrange("p (j q) -> p j q", j=AT)[:, :, t * P:(t + 1) * P]
                        nc.scalar.activation(dst, o4, ACT.Copy)
                        if t >= 1:
                            act.wait_ge(osq_ready, l * QT + t)
                        nc.scalar.activation(sq[:, :], bank(6), ACT.Square).then_inc(o_copied, 1)

                    if i == first_g - 1:
                        copy_scores(0); exps(0)
                    if i == first_g:
                        copy_scores(1); exps(1)
                    if i == first_g + 1:
                        copy_pt(0); copy_scores(2); exps(2)
                    if i == first_g + 2:
                        copy_out(0); copy_pt(1); copy_scores(3); exps(3)
                    if i == first_g + 3:
                        xcf = xc[:, :, :].rearrange("p a b -> p (a b)")
                        act.wait_ge(acc_act, proj_release(l, i)[1])
                        nc.scalar.activation(xcf, xcf, ACT.Gelu_apprx_tanh).then_inc(gelu_ready, 1)
                        fetch_sqrt()
                        copy_out(1); copy_pt(2); copy_out(2)
                        for j in range(LT):
                            act.wait_ge(l_ready, l * LT + j + 1)
                            nc.scalar.activation(I[:, j, :], yt(AT + j), ACT.Square).then_inc(lsq_ready, 1)
                        copy_out(3)
                sd_step(norm_no(l, 0), D_ATTN, 2)
                hi_tiles(conv_no(l, 0), mH, None)
                for j in range(NOUT):
                    n = B + NPROJ + j
                    split_step(n + 2, n % 2)
                    act.wait_ge(chunk_done, n + 1)
                    if j == 0:
                        act.wait_ge(lo_ready, conv_no(l, 0) + KT)
                    acc = bank(j % 2)
                    if j >= 2:
                        act.wait_ge(sq_used, sq_no(l, 0) + j - 1)
                    dst = ssq if j == 0 else sqb[j % 2]
                    nc.scalar.activation(dst, acc, ACT.Square).then_inc(sq_ready, 1)
                    nc.scalar.activation(yt(j), acc, ACT.Copy).then_inc(out_copied, 1)
                sd_step(norm_no(l, 1), D)
                x_norm(l, 1)
                hi_tiles(conv_no(l, 1), hH, mod[:, l * NMOD + 3, :])
                if l + 1 < DEPTH:
                    act.dma_start(gw[:, :, :], A["gw"][l + 1]).then_inc(gw_in, 16)

                for g in range(GROUPS):
                    G = B + NPROJ + NOUT + g * GSTEP
                    U = l * 2 * PAIRS + g * 2 * KT
                    Q = l * PAIRS + g * KT
                    with act.Fori(0, 2) as it:
                        for c in range(8):
                            n = it * 8 + G + c
                            u = it * 8 + U + c
                            pr = it * 4 + Q + c // 2
                            if c % 2:
                                act.wait_ge(f_taps, u + 4)
                                nc.scalar.activation(I[:, (c // 2) % 2, :], R[:, (c - 1) % 4, :],
                                                     ACT.Gelu_apprx_tanh).then_inc(f_gelu, 1)
                            act.wait_ge(chunk_done, n + 1)
                            col = it * 4 + (g * KT + c // 2 + (c % 2) * PAIRS)
                            nc.scalar.activation(
                                R[:, c % 4, :], bank(c % 4), ACT.Identity,
                                bias=par_l[:, bass.ds(col + COLS["fcb"], 1)],
                                scale=par_l[:, bass.ds(col + (COLS["fcw"] + 2 * 2 * PAIRS), 1)]).then_inc(f_base, 1)
                            split_step(n + 2, c % 2)
                            if c % 2:
                                act.wait_ge(f_mul, pr + 1)
                                nc.scalar.activation(mH[:, bass.ds(it * 4 + c // 2, 1), :].rearrange("p a b -> p (a b)"),
                                                     I[:, 2 + (c // 2) % 2, :], ACT.Copy).then_inc(act_hi, 1)
                    last_group = g == GROUPS - 1
                    V = G + 2 * KT
                    if last_group:
                        fetch_sqrt()
                    if not last_group:
                        with act.Fori(0, KT // 2) as it:
                            for c in range(2):
                                split_step(it * 2 + (V + c + 2), c % 2)
                    else:
                        for j in range(KT):
                            if V + j + 2 < DEPTH * NCH:
                                split_step(V + j + 2, j % 2)
                            squares_of(sq_no(l, 1), j, yt(j), dn_read, l * KT * GROUPS + g * KT + j + 1 + 2)
                sd_step(norm_no(l, 3), D)
                if l + 1 < DEPTH:
                    x_norm(l, 3)
                    hi_tiles(conv_no(l, 2), hH, mod[:, (l + 1) * NMOD, :])

        @block.vector
        def _(dve):
            V = Tally(dve_self)
            TT, TS, STT = nc.vector.tensor_tensor, nc.vector.tensor_scalar, nc.vector.scalar_tensor_tensor

            def self_wait():
                dve.wait_ge(dve_self, V.n)

            def link(ins):
                V.mark(ins)
                self_wait()

            def lo_chunk(n, parity):
                dve.wait_ge(w_hi, n + 1)
                TT(wL[:, parity, :], raw[:, parity, :], wH[:, parity, :].bitcast(fp32),
                   ALU.subtract).then_inc(w_lo, 1)

            def mac(u, slot, first, last, count):
                dve.wait_ge(ada_in[slot], count)
                cc = csil
                kt = slot_kt["kt"]
                if first:
                    ins = TS(macc[:, :], adaw[:, slot, :], cc[:, kt:kt + 1], None, ALU.mult)
                else:
                    ins = STT(out=macc[:, :], in0=adaw[:, slot, :], scalar=cc[:, kt:kt + 1], in1=macc[:, :],
                              op0=ALU.mult, op1=ALU.add)
                ins.then_inc(ada_used, 1)
                dve.wait_ge(ada_used, u + 1)
                if last:
                    dve.sem_inc(macc_ready, 1)

            slot_kt = {"kt": 0}

            def mac_unit(seg, kt):
                slot_kt["kt"] = kt
                if kt == 0:
                    if not (isinstance(seg, int) and seg == 0):
                        dve.wait_ge(mod_cols, seg + 0)
                u = seg * KT + kt
                mac(u, kt % 4, kt == 0, kt == KT - 1, (seg * 2 + kt // 4 + 1) * 16)

            def mod_store(seg, l_static, bcol):
                dve.wait_ge(mod_cols, seg + 1)
                V.mark(nc.vector.tensor_reduce(msum[:, :], bank(6, 2).rearrange("p (j q) -> p j q", j=KT),
                                               AX.X, ALU.add))
                self_wait()
                out = mod[:, seg, :] if isinstance(seg, int) else mod[:, bass.ds(seg, 1), :].rearrange("p a b -> p (a b)")
                TT(out, msum[:, :], bcol, ALU.add).then_inc(mod_done, 1)
                dve.wait_ge(mod_done, seg + 1)

            def mod_bias(seg):
                l, s = divmod(seg, NMOD)
                c = COLS["ada_b"] + s * KT
                return par[:, l, c:c + KT]

            def factors(l, which):
                seg, gain = [(1, "mix_pre"), (2, "mix_post"), (4, "ffn_pre"), (5, "ffn_post")][which]
                g = par[:, l, COLS[gain]:COLS[gain] + KT]
                m = mod[:, l * NMOD + seg, :]
                if which % 2 == 0:
                    link(STT(out=fac[:, l, which, :], in0=m, scalar=1.0, in1=g, op0=ALU.add, op1=ALU.mult))
                else:
                    link(TT(fac[:, l, which, :], m, g, ALU.mult))

            def make_rs(m, groups=1):
                if m in X_NORMS:
                    dve.wait_ge(sd_cols, X_NORMS.index(m) + 1)
                    nc.vector.reciprocal(rs8[:, 0:QT], bank(NORM_COLS)[:, 0:QT]).then_inc(rs_ready, 1)
                else:
                    dve.wait_ge(sd_ready, COL_NORMS.index(m) + 1)
                    n = groups * QT
                    nc.vector.reciprocal(rs8[:, 0:n], sd8[:, 0:n]).then_inc(rs_ready, 1)

            def add_square(m0, j):
                dve.wait_ge(sq_ready, m0 + j + 1)
                if j > 0:
                    TT(ssq, ssq, sqb[j % 2], ALU.add).then_inc(sq_used, 1)
                else:
                    dve.sem_inc(sq_used, 1)
                dve.wait_ge(sq_used, m0 + j + 1)
                if j == KT - 1:
                    dve.sem_inc(ssq_ready, 1)

            def split_tiles(k0, gains, rbs, dst, bias, x_of=None):
                def tmp(j):
                    if x_of:
                        dve.wait_ge(*x_new(*x_of, j))
                    STT(out=yt(j), in0=src(j), scalar=gains(j), in1=rbs(j), op0=ALU.mult,
                        op1=ALU.mult).then_inc(tmp_ready, 1)
                src = split_src["f"]
                tmp(0)
                for j in range(KT):
                    if j + 1 < KT:
                        tmp(j + 1)
                    dve.wait_ge(hi_ready, k0 + j + 1)
                    if bias is None:
                        TT(dst[:, j, :], yt(j), hi_of(dst)[:, j, :], ALU.subtract).then_inc(lo_ready, 1)
                    else:
                        STT(out=dst[:, j, :], in0=yt(j), scalar=bias[:, j:j + 1],
                            in1=hi_of(dst)[:, j, :], op0=ALU.add, op1=ALU.subtract).then_inc(lo_ready, 1)

            split_src = {"f": xt}

            def hi_of(dst):
                return (hH if dst is hL else mH)[:, :, :].bitcast(fp32)

            dve.sem_inc(f_taps, 4)
            dve.sem_inc(dn_read, 2)
            dve.wait_ge(early_in, 48)
            ang, turns = R[:, 0, :], R[:, 1, :]
            link(nc.vector.tensor_copy(R[:, 2, :], Adec[:, 0, :].bitcast(i32)))
            link(TS(ang, R[:, 2, :], freq, None, ALU.mult))
            for unit in (COARSE, 1.0):
                link(TS(turns, ang, 1.0 / (TWO_PI * unit), ROUND_MAGIC, ALU.mult, ALU.add))
                link(TS(turns, turns, ROUND_MAGIC, None, ALU.subtract))
                for part in PI_PARTS:
                    link(STT(out=ang, in0=turns, scalar=-part * unit, in1=ang, op0=ALU.mult, op1=ALU.add))
            PI = 3.1415925
            TS(ang, ang, PI, -PI, ALU.min, ALU.max).then_inc(ang_ready, 1)
            dve.wait_ge(c_exp, 1)
            link(TS(ctmp, ctmp, 1.0, None, ALU.add))
            link(nc.vector.reciprocal(ctmp, ctmp))
            link(TT(csil, craw, ctmp, ALU.mult))
            dve.wait_ge(sp_exp, 1)
            link(TS(sp1[:, :, :], sp2[:, :, :], 2.0, None, ALU.add))
            nc.vector.reciprocal(sp1[:, :, :], sp1[:, :, :]).then_inc(sp_recip, 1)
            for kt in range(KT):
                mac_unit(0, kt)
            dve.wait_ge(params_in, 16)
            for kt in range(KT):
                mac_unit(1, kt)
                if kt == 0:
                    mod_store(0, 0, mod_bias(0))
                if kt == KT // 2:
                    make_rs(0)
                if kt == KT - 3:
                    lo_chunk(0, 0)
                    lo_chunk(1, 1)
            mod_store(1, 0, mod_bias(1))
            factors(0, 0)
            dve.wait_ge(rb_ready, 1)
            split_tiles(0, lambda j: fac[:, 0, 0, j:j + 1], lambda j: bank(2), hL, mod[:, 0, :])

            for l in range(DEPTH):
                B = step_base(l)
                par_l = par[:, l, :]

                def extra(i):
                    for k in MAC_STEPS[l].get(i, []):
                        seg, kt = divmod(MAC_FIRST[l] + k, KT)
                        mac_unit(seg, kt)
                    if i in MOD_AT[l]:
                        seg = MOD_AT[l][i]
                        mod_store(seg, l, mod_bias(seg))

                def softmax(t):
                    sc = scores[t % 2].rearrange("p (s k) -> p s k", s=NQ)
                    m8, e8, d8 = mx[t % 2], es[t % 2], den[t % 2]
                    bc = lambda v: v.unsqueeze(2).broadcast_to([P, NQ, P])
                    sink = par_l[:, COLS["sink"]:COLS["sink"] + NQ]
                    dve.wait_ge(s_copied, l * QT + t + 1)
                    if t == 0:
                        link(nc.vector.memset(sc[0:CHUNK, :, 0:CHUNK], MASK))
                    link(nc.vector.tensor_reduce(m8, sc, AX.X, ALU.max))
                    link(TT(m8, m8, sink, ALU.max))
                    TT(e8, sink, m8, ALU.subtract)
                    TT(sc, sc, bc(m8), ALU.subtract).then_inc(s_sub, 1)
                    dve.wait_ge(s_exp, l * QT + t + 1)
                    link(nc.vector.tensor_reduce(d8, sc, AX.X, ALU.add))
                    link(TT(d8, d8, e8, ALU.add))
                    if t < QT - 1:
                        nc.vector.reciprocal(d8, d8).then_inc(den_ready, 1)
                    else:
                        link(nc.vector.reciprocal(d8, d8))
                        TT(sc, sc, bc(d8), ALU.mult).then_inc(p_last, 1)

                def out_squares(t):
                    dve.wait_ge(o_copied, l * QT + t + 1)
                    nc.vector.tensor_reduce(ssq[:, t * P:(t + 1) * P],
                                            sq[:, :].rearrange("p (j q) -> p q j", j=AT),
                                            AX.X, ALU.add).then_inc(osq_ready, 1)

                for i, kind in enumerate(PROJ):
                    n = B + i
                    lo_chunk(n + 2, n % 2)
                    acc = bank(i % 2)
                    if kind == "x":
                        dve.wait_ge(x_base, l * LT + i + 1)
                        for k in range(CONVW - 2, -1, -1):
                            back = CONVW - 1 - k
                            ins = STT(out=xc[:, i, back:], in0=acc[:, 0:SEQ - back],
                                      scalar=pcol(l, "lcw", k * LT + i), in1=xc[:, i, back:],
                                      op0=ALU.mult, op1=ALU.add)
                            if k:
                                link(ins)
                        ins.then_inc(acc_dve, 1)
                    elif kind in "kq":
                        j = i - LT
                        if l == 0 and kind == "k":
                            dve.wait_ge(rope_ready, 1)
                        dve.wait_ge(swap_ready, l * (AT + 1) + j + 1)
                        t1, t2 = scr[:, SEQ:2 * SEQ], scr[:, 0:SEQ]
                        V.mark(TT(t1, acc, cosT[:, :], ALU.mult))
                        link(TT(t2, t2, sinT[:, :], ALU.mult))
                        if kind == "q":
                            TT(yt(i - LT - 1), t1, t2, ALU.add).then_inc(acc_dve, 1)
                        else:
                            V.mark(TT(kd[0:HD, 0, CHUNK:], t1[0:HD], t2[0:HD], ALU.add))
                            link(TT(kd[HD:P, 1, CHUNK:], t1[HD:P], t2[HD:P], ALU.add))
                            nc.vector.tensor_copy(kd[HD:P, 0, CHUNK:], kd[0:HD, 0, CHUNK:])
                            nc.vector.tensor_copy(kd[0:HD, 1, CHUNK:], kd[HD:P, 1, CHUNK:]).then_inc(acc_dve, 1)
                            nc.vector.memset(vT[:, 0:CHUNK], 0.0).then_inc(v_pad, 1)
                    if i in (LT + 1, LT + 2):
                        for j in range(2 * (i - LT - 1), 2 * (i - LT - 1) + 2):
                            dve.wait_ge(aT_ready, l * LT + j + 1)
                            V.mark(TT(I[:, j, :], I[:, j, :], xc[:, j, :], ALU.mult))
                            link(STT(out=R[:, j, :], in0=Adec[:, j, :], scalar=1.0, in1=R[:, j, :],
                                     op0=ALU.add, op1=ALU.mult))
                            link(TS(Adec[:, j, :], R[:, j, :], -1.0, 1.0, ALU.mult, ALU.add))
                            STT(out=R[:, j, :], in0=Adec[:, j, :], scalar=1.0, in1=R[:, j, :],
                                op0=ALU.add, op1=ALU.mult).then_inc(b2_ready, 1)
                    if i == LT + 4:
                        dve.wait_ge(root_ready, l + 1)
                        dve.wait_ge(b2_ready, (l + 1) * LT)
                        If = I[:, :, :].rearrange("p a b -> p (a b)")
                        link(TT(If, If, Rf, ALU.mult))
                    if i == LT + 5:
                        for j in range(LT):
                            nc.vector.tensor_tensor_scan(yt(AT + j), Adec[:, j, :], I[:, j, :], 0.0,
                                                         ALU.mult, ALU.add).then_inc(scan_done, 1)
                    extra(i)
                    t = i - (NPROJ - LT - 1)
                    if 0 <= t < QT:
                        softmax(t)
                out_squares(0)
                out_squares(1)
                dve.wait_ge(pt_mm, (l + 1) * QT)
                dve.wait_ge(o_mm, l * QT + QT - 2)
                nc.vector.tensor_copy(probsT[(QT - 1) % 2], bank(4, 2)).then_inc(pt_last, 1)
                out_squares(2)
                dve.wait_ge(lsq_ready, l * LT + 2)
                link(TT(I[:, 0, :], I[:, 0, :], I[:, 1, :], ALU.add))
                for j in range(2, LT):
                    dve.wait_ge(lsq_ready, l * LT + j + 1)
                    link(TT(I[:, 0, :], I[:, 0, :], I[:, j, :], ALU.add))
                out_squares(QT - 1)
                dve.wait_ge(osq_ready, (l + 1) * QT)
                dve.sem_inc(ssq_ready, 1)
                make_rs(norm_no(l, 0), 2)
                dve.wait_ge(rb_ready, norm_no(l, 0) + 1)
                split_src["f"] = yt
                split_tiles(conv_no(l, 0),
                            lambda j: pcol(l, "g_attn", j) if j < AT else pcol(l, "g_lru", j - AT),
                            lambda j: bank(2 if j < AT else 3), mL, None)
                for j in range(NOUT):
                    n = B + NPROJ + j
                    lo_chunk(n + 2, n % 2)
                    add_square(sq_no(l, 0), j)
                    extra(NPROJ + j)

                def scale_y(which, k):
                    rb = bank(RB_BANK[k])
                    for j in range(KT):
                        STT(out=yt(j), in0=yt(j), scalar=fac[:, l, which, j:j + 1], in1=rb,
                            op0=ALU.mult, op1=ALU.mult).then_inc(y_scaled, 1)
                        if j in X_DVE:
                            dve.wait_ge(y_scaled, (2 * l + k // 2) * KT + j + 1)
                            TT(xt(j), xt(j), yt(j), ALU.add).then_inc(x_done2, 1)

                factors(l, 1)
                make_rs(norm_no(l, 1))
                dve.wait_ge(rb_ready, norm_no(l, 1) + 1)
                dve.wait_ge(out_copied, (l + 1) * NOUT)
                scale_y(1, 1)
                factors(l, 2)
                make_rs(norm_no(l, 2))
                dve.wait_ge(rb_ready, norm_no(l, 2) + 1)
                split_src["f"] = xt
                split_tiles(conv_no(l, 1), lambda j: fac[:, l, 2, j:j + 1], lambda j: bank(RB_BANK[2]),
                            hL, mod[:, l * NMOD + 3, :], (l, 0))

                for g in range(GROUPS):
                    G = B + NPROJ + NOUT + g * GSTEP
                    U = l * 2 * PAIRS + g * 2 * KT
                    Q = l * PAIRS + g * KT
                    start, marks = V.n, V.marks
                    PER = 8 + (l == 0)
                    with dve.Fori(0, 2) as it:
                        V.n = it * PER + start
                        for c in range(8):
                            n = it * 8 + G + c
                            u = it * 8 + U + c
                            dve.wait_ge(f_base, u + 1)
                            col = it * 4 + (g * KT + c // 2 + (c % 2) * PAIRS)
                            buf, acc = R[:, c % 4, :], bank(c % 4)
                            link(STT(out=buf[:, 1:], in0=acc[:, 0:SEQ - 1],
                                     scalar=par_l[:, bass.ds(col + (COLS["fcw"] + 2 * PAIRS), 1)],
                                     in1=buf[:, 1:], op0=ALU.mult, op1=ALU.add))
                            STT(out=buf[:, 2:], in0=acc[:, 0:SEQ - 2],
                                scalar=par_l[:, bass.ds(col + COLS["fcw"], 1)],
                                in1=buf[:, 2:], op0=ALU.mult, op1=ALU.add).then_inc(f_taps, 1)
                            if c % 2:
                                pr, p = it * 4 + Q + c // 2, c // 2
                                dve.wait_ge(f_gelu, pr + 1)
                                dve.wait_ge(f_taps, u + 5)
                                TT(I[:, 2 + p % 2, :], I[:, p % 2, :], buf, ALU.mult).then_inc(f_mul, 1)
                            lo_chunk(n + 2, c % 2)
                            if c % 2:
                                dve.wait_ge(act_hi, pr + 1)
                                at = bass.ds(it * 4 + p, 1)
                                TT(mL[:, at, :].rearrange("p a b -> p (a b)"), I[:, 2 + p % 2, :],
                                   mH[:, at, :].rearrange("p a b -> p (a b)").bitcast(fp32),
                                   ALU.subtract).then_inc(act_lo, 1)
                            if l == 0:
                                for kt in UP_MACS.get(c, []):
                                    mac_unit(it + (NMOD - 1 + 2 * g), kt)
                        if l == 0:
                            seg = it + (NMOD - 1 + 2 * g)
                            bl, bs = divmod(NMOD - 1 + 2 * g, NMOD)
                            if g == 0:
                                bcol = par[:, :, :].rearrange("p l c -> p (l c)")[
                                    :, bass.ds(it * (NPAR - (NMOD - 1) * KT) + (COLS["ada_b"] + (NMOD - 1) * KT), KT)]
                            else:
                                bcol = par[:, bl, :][:, bass.ds(it * KT + (COLS["ada_b"] + bs * KT), KT)]
                            mod_store(seg, l, bcol)
                    assert V.marks - marks == PER, V.marks - marks
                    V.n = start + 2 * PER
                    VD = G + 2 * KT
                    DN = l * GROUPS * KT + g * KT

                    def down(n, j, c, dn):
                        if not (isinstance(n, int) and n + 2 >= DEPTH * NCH):
                            lo_chunk(n + 2, c)
                        dve.wait_ge(chunk_done, n + 1)
                        acc = bank(4 + c)
                        out = yt(j) if isinstance(j, int) else y[:, :].rearrange("p (j q) -> p j q", j=KT)[
                            :, bass.ds(j, 1), :].rearrange("p a b -> p (a b)")
                        if g == 0:
                            nc.vector.tensor_copy(out, acc).then_inc(dn_read, 1)
                        else:
                            TT(out, acc, out, ALU.add).then_inc(dn_read, 1)

                    if g < GROUPS - 1:
                        with dve.Fori(0, KT // 2) as it:
                            for c in range(2):
                                down(it * 2 + (VD + c), it * 2 + c, c, None)
                    else:
                        for j in range(KT):
                            down(VD + j, j, j % 2, None)
                            if j:
                                add_square(sq_no(l, 1), j - 1)
                        add_square(sq_no(l, 1), KT - 1)
                factors(l, 3)
                make_rs(norm_no(l, 3))
                dve.wait_ge(rb_ready, norm_no(l, 3) + 1)
                scale_y(3, 3)
                if l + 1 < DEPTH:
                    factors(l + 1, 0)
                    make_rs(norm_no(l, 4))
                    dve.wait_ge(rb_ready, norm_no(l, 4) + 1)
                    split_src["f"] = xt
                    split_tiles(conv_no(l, 2), lambda j: fac[:, l + 1, 0, j:j + 1],
                                lambda j: bank(RB_BANK[4]), hL, mod[:, (l + 1) * NMOD, :], (l, 1))

        @block.tensor
        def _(pe):
            def mm(out, a, b, start, stop, **kw):
                return nc.tensor.matmul(out, a, b, start=start, stop=stop, **kw)

            def tile_products(acc, slot, hi_, lo_, ready):
                for kt in range(KT):
                    if ready:
                        ready(kt)
                    a, al = wH[:, slot, kt * P:(kt + 1) * P], wL[:, slot, kt * P:(kt + 1) * P]
                    mm(acc, a, hi_[:, kt, :], kt == 0, False)
                    mm(acc, a, lo_[:, kt, :], False, False)
                    last = mm(acc, al, hi_[:, kt, :], False, kt == KT - 1)
                last.then_inc(chunk_done, 1)

            def norm_cols(m, mods, also=None):
                if m == 0:
                    pe.wait_ge(presq_used, KT - 1)
                else:
                    pe.wait_ge(ssq_ready, COL_NORMS.index(m))
                if mods:
                    pe.wait_ge(mod_done, mods)
                for g, src in enumerate([ssq] if also is None else [ssq, also]):
                    for t in range(QT):
                        last = mm(bank(NORM_COLS)[:, g * QT + t:g * QT + t + 1], src[:, t * P:(t + 1) * P],
                                  ones[:, 0:1], True, True)
                last.then_inc(cols_ready, 1)

            def keep_clock(n):
                for _ in range(n):
                    mm(bank(SPARE)[:, 0:P], ident[:, :], ident[:, :], True, True)

            def x_sum(m):
                i = X_NORMS.index(m)
                keep_clock(8)
                for j in range(KT):
                    pe.wait_ge(xsq_ready, i * KT + j + 1)
                    ins = mm(bank(XSUM), ones[:, :], xsqb[j % 4], j == 0, j == KT - 1)
                    ins.then_inc(xsq_used if j < KT - 1 else xsum_ready, 1)
                pe.wait_ge(sd_row, i + 1)
                for t in range(QT):
                    last = mm(bank(NORM_COLS)[:, t:t + 1], ssq[0:1, t * P:(t + 1) * P], ones[0:1, 0:1], True, True)
                last.then_inc(sd_cols, 1)

            def norm_spread(m, b, groups=1):
                pe.wait_ge(rs_ready, m + 1)
                for g in range(groups):
                    for t in range(QT):
                        last = mm(bank(b + g)[:, t * P:(t + 1) * P],
                                  rs8[:, g * QT + t:g * QT + t + 1].broadcast_to([P, P]), ident[:, :], True, True)
                last.then_inc(rb_ready, 1)

            def mod_sum(seg, norms):
                pe.wait_ge(macc_ready, seg + 1)
                if norms:
                    pe.wait_ge(rs_ready, norms)
                if not (isinstance(seg, int) and seg == 0):
                    pe.wait_ge(mod_done, seg + 0)
                for j in range(KT):
                    last = nc.tensor.transpose(bank(6, 2)[:, j * P:(j + 1) * P], macc[:, j * P:(j + 1) * P],
                                               ident[:, :])
                last.then_inc(mod_cols, 1)

            pe.wait_ge(consts, NCONST)
            mod_sum(0, 0)
            norm_cols(0, 1)
            norm_spread(0, 2)
            mod_sum(1, 1)

            for l in range(DEPTH):
                B = step_base(l)

                def gates(j):
                    rel, val = proj_release(l, j)
                    pe.wait_ge(rel, val)
                    if j >= 2:
                        pe.wait_ge(sig_done, l * LT + j - 1)
                    if j == 0:
                        pe.wait_ge(gw_in, 16 * (l + 1))
                    b = 2 + 2 * (j % 2)
                    mm(bank(b), gw[:, j, :], xc[:, j, :], True, True)
                    mm(bank(b + 1), gw[:, LT + j, :], xc[:, j, :], True, True).then_inc(gate_mm, 1)

                def values():
                    pe.wait_ge(*proj_release(l, NPROJ - LT - 1))
                    pe.wait_ge(sig_done, (l + 1) * LT)
                    for w in range(SEQ // CHUNK):
                        last = nc.tensor.transpose(bank(4, 2)[:, w * P:(w + 1) * P],
                                                   vT[:, w * CHUNK:w * CHUNK + P], ident[:, :])
                    last.then_inc(vw_mm, 1)

                def scores_mm(t):
                    if t == 0:
                        rel, val = proj_release(l, NPROJ - LT - 2)
                        pe.wait_ge(rel, val)
                    else:
                        pe.wait_ge(s_copied, l * QT + t)
                    for s in range(NQ):
                        h = SLOTS[s]
                        at = HD * (h % 2)
                        for half in range(2):
                            w = (2 * t + half) * CHUNK
                            last = mm(bank(2, 2)[half * CHUNK:(half + 1) * CHUNK, s * P:(s + 1) * P],
                                      yt(h // 2)[at:at + HD, w:w + CHUNK],
                                      kd[at:at + HD, h // (NQ // NKV), w:w + P], True, True)
                    last.then_inc(s_mm, 1)

                def probs_transposed(t):
                    if t < QT - 1:
                        pe.wait_ge(p_ready, l * (QT - 1) + t + 1)
                    else:
                        pe.wait_ge(p_last, l + 1)
                    if t == 0:
                        pe.wait_ge(vw_ready, l + 1)
                    else:
                        pe.wait_ge(pt_copied, l * (QT - 1) + t)
                    for s in range(NQ):
                        last = nc.tensor.transpose(bank(4, 2)[:, s * P:(s + 1) * P],
                                                   scores[t % 2][:, s * P:(s + 1) * P], ident[:, :])
                    last.then_inc(pt_mm, 1)

                def outputs_mm(t):
                    if t < QT - 1:
                        pe.wait_ge(pt_copied, l * (QT - 1) + t + 1)
                    else:
                        pe.wait_ge(pt_last, l + 1)
                    if t:
                        pe.wait_ge(o_copied, l * QT + t)
                    pt = probsT[t % 2].rearrange("p (s q) -> p s q", s=NQ)
                    o4 = bank(6).rearrange("p (j q) -> p j q", j=AT)
                    for kv in range(NKV):
                        for half in range(2):
                            for odd in range(2):
                                last = mm(o4[HD * odd:HD * (odd + 1), 2 * kv:2 * kv + 2,
                                             half * CHUNK:(half + 1) * CHUNK],
                                          vw[:, 2 * t + half, kv * HD:(kv + 1) * HD],
                                          pt[:, 4 * odd + 2 * kv:4 * odd + 2 * kv + 2,
                                             half * CHUNK:(half + 1) * CHUNK], True, True)
                    last.then_inc(o_mm, 1)

                for i, kind in enumerate(PROJ):
                    n = B + i
                    pe.wait_ge(w_lo, n + 1)
                    if i >= 2:
                        pe.wait_ge(*proj_release(l, i - 2))
                    k0 = 0 if l == 0 else conv_no(l - 1, 2)
                    ready = (lambda kt: pe.wait_ge(lo_ready, k0 + kt + 1)) if i == 0 else None
                    tile_products(bank(i % 2), n % 2, hH, hL, ready)
                    if 1 <= i <= LT:
                        gates(i - 1)
                    first_g = NPROJ - LT
                    if i == first_g - 1:
                        scores_mm(0)
                    if i == first_g:
                        values()
                        scores_mm(1)
                    if i == first_g + 1:
                        probs_transposed(0)
                        scores_mm(2)
                    if i == first_g + 2:
                        outputs_mm(0)
                        probs_transposed(1)
                        scores_mm(3)
                    if i == first_g + 3:
                        outputs_mm(1)
                        probs_transposed(2)
                        outputs_mm(2)
                        probs_transposed(3)
                        outputs_mm(3)
                    if i in MOD_AT[l]:
                        mod_sum(MOD_AT[l][i], norm_no(l, 0))
                mods = 3 if l == 0 else 11
                norm_cols(norm_no(l, 0), mods, I[:, 0, :])
                norm_spread(norm_no(l, 0), RB_BANK[0], 2)
                for j in range(NOUT):
                    n = B + NPROJ + j
                    pe.wait_ge(w_lo, n + 1)
                    if j < 2:
                        pe.wait_ge(*proj_release(l, NPROJ - 2 + j))
                    else:
                        pe.wait_ge(out_copied, l * NOUT + j - 1)
                    ready = (lambda kt: pe.wait_ge(lo_ready, conv_no(l, 0) + kt + 1)) if j == 0 else None
                    tile_products(bank(j % 2), n % 2, mH, mL, ready)
                    if NPROJ + j in MOD_AT[l]:
                        mod_sum(MOD_AT[l][NPROJ + j], norm_no(l, 1))
                mods = 5 if l == 0 else 12
                norm_cols(norm_no(l, 1), mods)
                norm_spread(norm_no(l, 1), RB_BANK[1])
                x_sum(norm_no(l, 2))
                norm_spread(norm_no(l, 2), RB_BANK[2])
                for g in range(GROUPS):
                    G = B + NPROJ + NOUT + g * GSTEP
                    U = l * 2 * PAIRS + g * 2 * KT
                    with pe.Fori(0, 2) as it:
                        for c in range(8):
                            pe.wait_ge(w_lo, it * 8 + (G + c + 1))
                            pe.wait_ge(f_taps, it * 8 + (U + c + 1))
                            ready = (lambda kt: pe.wait_ge(lo_ready, conv_no(l, 1) + kt + 1)) if c == 0 else None
                            tile_products(bank(c % 4), c % 2, hH, hL, ready)
                        if l == 0:
                            mod_sum(it + (NMOD - 1 + 2 * g), norm_no(l, 3))
                    DN = l * GROUPS * KT + g * KT
                    VD = G + 2 * KT
                    with pe.Fori(0, KT // 2) as it:
                        for c in range(2):
                            pe.wait_ge(w_lo, it * 2 + (VD + c + 1))
                            pe.wait_ge(dn_read, it * 2 + (DN + c + 1))
                            ready = (lambda kt: pe.wait_ge(act_lo, l * PAIRS + g * KT + kt + 1)) if c == 0 else None
                            tile_products(bank(4 + c), c, mH, mL, ready)
                mods = 11 if l == 0 else 12
                norm_cols(norm_no(l, 3), mods)
                norm_spread(norm_no(l, 3), RB_BANK[3])
                if l + 1 < DEPTH:
                    x_sum(norm_no(l, 4))
                    norm_spread(norm_no(l, 4), RB_BANK[4])


def columns(a):
    a = np.asarray(a)
    return np.swapaxes(a.reshape(*a.shape[:-1], a.shape[-1] // P, P), -1, -2)


def kernel(**inputs):
    import concourse.bacc as bacc
    from concourse.bass_utils import run_bass_kernel_spmd

    a = {k: np.asarray(v) for k, v in inputs.items()}
    L = DEPTH

    def tiles(w, n_k):
        w = w.reshape(n_k, P, w.shape[1] // P, P)
        return w.transpose(2, 1, 0, 3)
    stream = np.empty((L, NCH, P, KT, P), np.float32)
    kv = NKV * HD
    starts = {"q": 0, "k": D_ATTN, "v": D_ATTN + kv, "x": D_ATTN + 2 * kv, "g": D_ATTN + 2 * kv + D_LRU}
    for l in range(L):
        w_in = tiles(a["w_in"][l], KT)
        seen = dict.fromkeys(starts, 0)
        for i, kind in enumerate(PROJ):
            stream[l, i] = w_in[starts[kind] // P + seen[kind]]
            seen[kind] += 1
        stream[l, NPROJ:NPROJ + NOUT] = tiles(a["w_out"][l], KT)
        up = tiles(a["ffn_w_up"][l], KT)
        down = tiles(a["ffn_w_down"][l], PAIRS)
        at = NPROJ + NOUT
        for g in range(GROUPS):
            for i in range(KT):
                stream[l, at] = up[g * KT + i]
                stream[l, at + 1] = up[PAIRS + g * KT + i]
                at += 2
            stream[l, at:at + KT] = down[:, :, g * KT:(g + 1) * KT, :]
            at += KT
    stream = stream.reshape(L * NCH, P, KT * P)

    ada = a["ada_w"].reshape(L, KT, P, NMOD, D).transpose(0, 3, 1, 2, 4)
    ada = np.ascontiguousarray(ada).reshape(L * NMOD * KT, P, D)

    gw = np.zeros((L, P, 2 * LT, P), np.float32)
    for which, name in enumerate(("lru_w_a", "lru_w_x")):
        w = a[name]
        for j in range(LT):
            for b in range(2):
                s = slice(b * 64, b * 64 + 64)
                gw[:, s, which * LT + j, s] = w[:, 2 * j + b]

    par = np.empty((L, P, NPAR), np.float32)

    def put(name, cols):
        par[:, :, COLS[name]:COLS[name] + cols.shape[-1]] = cols
    for name, key in [("mix_pre", "mix_pre_g"), ("mix_post", "mix_post_g"), ("ffn_pre", "ffn_pre_g"),
                      ("ffn_post", "ffn_post_g"), ("g_attn", "grp_g_attn"), ("g_lru", "grp_g_lru"),
                      ("lcb", "lru_conv_b"), ("ba", "lru_b_a"), ("bx", "lru_b_x"), ("lam", "lru_lambda"),
                      ("fcb", "ffn_conv_b"), ("ada_b", "ada_b")]:
        put(name, columns(a[key]))
    put("lcw", columns(a["lru_conv_w"].reshape(L, CONVW * D_LRU)))
    put("fcw", columns(a["ffn_conv_w"].reshape(L, FCONV * 2 * DFF)))
    put("sink", np.broadcast_to(a["attn_sinks"][:, None, SLOTS], (L, P, NQ)))

    half = HD // 2
    inv = (THETA ** (-np.arange(0, HD, 2, dtype=np.float64) / HD)).astype(np.float32)
    arrays = {
        "in_w": stream, "in_ada": ada, "in_gw": gw, "in_par": par,
        "in_x": np.ascontiguousarray(a["x"][0].reshape(SEQ, KT, P).transpose(2, 1, 0)).reshape(P, KT * SEQ),
        "in_c": np.ascontiguousarray(columns(a["c"][0])),
        "in_pos": np.ascontiguousarray(np.broadcast_to(a["positions"][0][None, :], (P, SEQ))),
        "in_inv_freq": np.tile(inv, P // half).reshape(P, 1),
    }
    nc = bacc.Bacc("TRN2", target_bir_lowering=False, num_devices=1)
    A = {}
    for name, arr in arrays.items():
        A[name[3:]] = nc.dram_tensor(name, arr.shape, mybir.dt.from_np(arr.dtype), kind="ExternalInput").ap()
    A["out"] = nc.dram_tensor("out_0", (P, KT * SEQ), mybir.dt.float32, kind="ExternalOutput").ap()
    build(nc, A)
    r = run_bass_kernel_spmd(nc, [arrays], core_ids=[0])
    out = r.results[0]["out_0"]
    return np.ascontiguousarray(out.reshape(P, KT, SEQ).transpose(2, 1, 0)).reshape(1, SEQ, D)
```

```python
import numpy as np
import concourse.bass as bass
from concourse import mybir
from contextlib import ExitStack

P = 128
DEPTH, SEQ, D = 2, 512, 1024
CHUNK, HD, NQ, NKV = 64, 64, 8, 2
D_ATTN, D_LRU = 512, 512
DFF = 3072
EPS = 1e-6
MASK = -1e30
THETA = 10000.0
KT = D // P
AT, LT = D_ATTN // P, D_LRU // P
QT = SEQ // P
PAIRS = DFF // P
GROUPS = PAIRS // KT
PROJ = ["x"] * LT + ["k"] + ["q"] * AT + ["v"] + ["g"] * LT
NPROJ = len(PROJ)
NOUT = KT
GSTEP = 3 * KT
NCH = NPROJ + NOUT + GROUPS * GSTEP
NMOD = 6
CONVW = 4
FCONV = 3
SLOTS = [2 * (s % 4) + s // 4 for s in range(NQ)]

COLS = {}
_at = 0
for _name, _n in [("mix_pre", KT), ("mix_post", KT), ("ffn_pre", KT), ("ffn_post", KT),
                  ("g_attn", AT), ("g_lru", LT), ("lcw", CONVW * LT), ("lcb", LT), ("ba", LT),
                  ("bx", LT), ("lam", LT), ("fcw", FCONV * 2 * PAIRS), ("fcb", 2 * PAIRS),
                  ("ada_b", NMOD * KT), ("sink", NQ)]:
    COLS[_name] = _at
    _at += _n
NPAR = _at

TWO_PI = 6.283185307179586
def _parts(value, bits, n):
    out = []
    for i in range(n):
        if i == n - 1:
            out.append(float(np.float32(value)))
        else:
            q = 2.0 ** (np.floor(np.log2(value)) - bits + 1)
            part = float(np.floor(value / q) * q)
            out.append(part)
            value -= part
    return out
PI_PARTS = _parts(TWO_PI, 11, 3)
ROUND_MAGIC = float(1.5 * 2 ** 23)
COARSE = 1024.0


class Tally:

    def __init__(self, sem):
        self.sem, self.n, self.marks = sem, 0, 0

    def mark(self, instruction):
        instruction.then_inc(self.sem, 1)
        self.n = self.n + 1
        self.marks += 1


def build(nc, A):
    fp32, fp32r, i32 = mybir.dt.float32, mybir.dt.float32r, mybir.dt.int32
    ALU, ACT, AX = mybir.AluOpType, mybir.ActivationFunctionType, mybir.AxisListType
    ctx = ExitStack()
    with ctx:
        def sb(name, shape, dt=fp32):
            return ctx.enter_context(nc.sbuf_tensor("sb_" + name, shape, dt))

        def sem(name):
            return ctx.enter_context(nc.semaphore(name))

        x = sb("x", [P, KT * SEQ])
        hH = sb("hH", [P, KT, SEQ], fp32r)
        hL = sb("hL", [P, KT, SEQ], fp32r)
        mH = sb("mH", [P, KT, SEQ], fp32r)
        mL = sb("mL", [P, KT, SEQ], fp32r)
        y = sb("y", [P, KT * SEQ])
        raw = sb("raw", [P, 2, KT * P])
        wH = sb("wH", [P, 2, KT * P], fp32r)
        wL = sb("wL", [P, 2, KT * P], fp32r)
        adaw = sb("adaw", [P, 4, D])
        macc = sb("macc", [P, D])
        par = sb("par", [P, DEPTH, NPAR])
        mod = sb("mod", [P, DEPTH * NMOD, KT])
        fac = sb("fac", [P, DEPTH, 4, KT])
        gw = sb("gw", [P, 2 * LT, P])
        ones = sb("ones", [P, P])
        ident = sb("ident", [P, P])
        R = sb("R", [P, 4, SEQ])
        I = sb("I", [P, 4, SEQ])
        Adec = sb("Adec", [P, 4, SEQ])
        xc = sb("xc", [P, 4, SEQ])
        kd = sb("kd", [P, NKV, CHUNK + SEQ])
        vw = sb("vw", [P, 8, P])
        scr = sb("scr", [P, 2 * SEQ])
        work = sb("work", [P, 2 * SEQ])
        cosT = sb("cosT", [P, SEQ])
        sinT = sb("sinT", [P, SEQ])
        sq = sb("sq", [P, SEQ])
        ssqv = sb("ssqv", [P, CHUNK + SEQ])
        ssq = ssqv[:, 0:SEQ]
        msum = sb("msum", [P, KT])
        tiny = sb("tiny", [P, 96])

        ps = ctx.enter_context(nc.psum_tensor("ps", [P, 8 * SEQ], fp32))

        def bank(b, n=1):
            return ps[:, b * SEQ:(b + n) * SEQ]

        def xt(j):
            return x[:, j * SEQ:(j + 1) * SEQ]

        def yt(j):
            return y[:, j * SEQ:(j + 1) * SEQ]

        vT = ssqv[:, :]
        Rf = R[:, :, :].rearrange("p a b -> p (a b)")
        scores = [work[:, :], Rf[:, 0:2 * SEQ]]
        probsT = [scr[:, :], Rf[:, 2 * SEQ:4 * SEQ]]
        sqb = [sq[:, :], work[:, SEQ:2 * SEQ]]
        xsqb = [sq[:, :], work[:, SEQ:2 * SEQ], work[:, 0:SEQ], ssq]
        def cols_bank(m):
            return bank(2 if m in (norm_no(0, 1), norm_no(1, 1)) else 7)

        def pcol(l, name, i=0):
            c = COLS[name] + i
            return par[:, l, c:c + 1]

        mx = [tiny[:, 0:8], tiny[:, 8:16]]
        den = [tiny[:, 16:24], tiny[:, 24:32]]
        es = [tiny[:, 32:40], tiny[:, 40:48]]
        eps = tiny[:, 56:57]
        sign = tiny[:, 57:58]
        freq = tiny[:, 58:59]
        sd8 = tiny[:, 48:56]
        rs8 = tiny[:, 88:96]
        csil = tiny[:, 64:72]
        craw = tiny[:, 72:80]
        ctmp = tiny[:, 80:88]
        spl = sb("spl", [P, DEPTH, LT])
        nspl = sb("nspl", [P, DEPTH, LT])
        sp1 = sb("sp1", [P, DEPTH, LT])
        sp2 = sb("sp2", [P, DEPTH, LT])
        sp3 = sb("sp3", [P, DEPTH, LT])

        w_in = [sem("w_in0"), sem("w_in1")]
        w_hi, w_lo = sem("w_hi"), sem("w_lo")
        chunk_done = sem("chunk_done")
        ada_in = [sem(f"ada_in{i}") for i in range(4)]
        ada_used = sem("ada_used")
        macc_ready, mod_cols, mod_done = sem("macc_ready"), sem("mod_cols"), sem("mod_done")
        early_in, params_in, gw_in = sem("early_in"), sem("params_in"), sem("gw_in")
        x_in = [sem("x_in0"), sem("x_in1")]
        consts = sem("consts")
        dve_self, act_self = sem("dve_self"), sem("act_self")
        c_exp, sp_exp, sp_recip, sp_ready = sem("c_exp"), sem("sp_exp"), sem("sp_recip"), sem("sp_ready")
        presq_ready, presq_used, pool_self = sem("presq_ready"), sem("presq_used"), sem("pool_self")
        ang_ready, sin_ready, rope_ready = sem("ang_ready"), sem("sin_ready"), sem("rope_ready")
        ssq_ready, cols_ready, sd_ready = sem("ssq_ready"), sem("cols_ready"), sem("sd_ready")
        lru_summed = sem("lru_summed")
        rs_ready, rb_ready = sem("rs_ready"), sem("rb_ready")
        xsq_ready, xsq_used, sd_row, sd_cols = sem("xsq_ready"), sem("xsq_used"), sem("sd_row"), sem("sd_cols")
        xsum_ready, x_done2 = sem("xsum_ready"), sem("x_done2")
        sq_ready, sq_used = sem("sq_ready"), sem("sq_used")
        tmp_ready, hi_ready, lo_ready = sem("tmp_ready"), sem("hi_ready"), sem("lo_ready")
        pool_hi, lo_ready2 = sem("pool_hi"), sem("lo_ready2")
        x_done, y_scaled = sem("x_done"), sem("y_scaled")
        den_ready, scan_done, pt_last = sem("den_ready"), sem("scan_done"), sem("pt_last")
        p_last = sem("p_last")
        x_base, acc_dve, acc_act = sem("x_base"), sem("acc_dve"), sem("acc_act")
        swap_ready, v_pad = sem("swap_ready"), sem("v_pad")
        gate_mm, sig_done, aT_ready, b2_ready = sem("gate_mm"), sem("sig_done"), sem("aT_ready"), sem("b2_ready")
        root_ready, gated_ready, drive_ready = sem("root_ready"), sem("gated_ready"), sem("drive_ready")
        vw_mm, vw_ready = sem("vw_mm"), sem("vw_ready")
        s_mm, s_sub, s_exp, p_ready = sem("s_mm"), sem("s_sub"), sem("s_exp"), sem("p_ready")
        pt_mm, pt_copied, o_mm, o_copied, osq_ready = sem("pt_mm"), sem("pt_copied"), sem("o_mm"), sem("o_copied"), sem("osq_ready")
        gelu_ready, l_ready, lsq_ready = sem("gelu_ready"), sem("l_ready"), sem("lsq_ready")
        out_copied = sem("out_copied")
        f_base, f_taps, f_gelu, f_mul = sem("f_base"), sem("f_taps"), sem("f_gelu"), sem("f_mul")
        act_hi, act_lo, dn_read = sem("act_hi"), sem("act_lo"), sem("dn_read")
        stored = sem("stored")
        block = ctx.enter_context(nc.Block())

        NORMS = 5
        def norm_no(l, k):
            return 1 + l * NORMS + k
        X_NORMS = [norm_no(0, 2), norm_no(0, 4), norm_no(1, 2)]
        COL_NORMS = [m for m in range(norm_no(1, 3) + 1) if m not in X_NORMS]
        XSUM = 0
        X_DVE = [0, 2, 5, 7]
        X_POOL = [j for j in range(KT) if j not in X_DVE]
        def x_new(l, k, j):
            mine, s_ = (X_DVE, x_done2) if j in X_DVE else (X_POOL, x_done)
            return s_, (2 * l + k) * len(mine) + mine.index(j) + 1
        RB_BANK = [2, 4, 5, 6, 2]
        def conv_no(l, k):
            return KT + l * 3 * KT + k * KT
        LO_POOL = [1, 3, 5, 6]
        LO_DVE = [j for j in range(KT) if j not in LO_POOL]
        def lo_part(k0, j):
            mine, s_ = (LO_POOL, lo_ready2) if j in LO_POOL else (LO_DVE, lo_ready)
            return s_, k0 // KT * len(mine) + mine.index(j) + 1
        presq = [work[:, 0:SEQ], work[:, SEQ:2 * SEQ], sq[:, :]]
        def sq_no(l, k):
            return l * 2 * KT + k * KT

        def proj_release(l, i):
            dve_kinds = "xkq"
            if PROJ[i] in dve_kinds:
                per = sum(k in dve_kinds for k in PROJ)
                return acc_dve, l * per + sum(k in dve_kinds for k in PROJ[:i + 1])
            per = sum(k not in dve_kinds for k in PROJ)
            return acc_act, l * per + sum(k not in dve_kinds for k in PROJ[:i + 1])

        MAC_STEPS = {0: {0: [0, 1], 1: [2], 2: [3], 3: [4], 4: [5], 7: [6], 8: [7],
                         14: [8, 9, 10], 15: [11, 12], 16: [13, 14, 15], 17: [16, 17],
                         18: [18, 19], 19: [20, 21], 20: [22, 23]},
                     1: {14 + i: [i] for i in range(4)} | {18: [4, 5], 19: [6, 7]}}
        MAC_FIRST = {0: 2 * KT, 1: 11 * KT}
        MOD_AT = {0: {9: 2, 17: 3, 21: 4}, 1: {20: 11}}
        UP_MACS = {0: [0, 1], 1: [2], 2: [3, 4], 3: [5], 4: [6], 5: [7]}

        def step_base(l):
            return l * NCH

        @block.sync
        def _(sp):
            sp.dma_start(craw, A["c"]).then_inc(early_in, 16)
            sp.dma_start(freq, A["inv_freq"]).then_inc(early_in, 16)
            sp.dma_start(Adec[:, 0, :].bitcast(i32), A["pos"]).then_inc(early_in, 16)
            sp.dma_start(par[:, :, :], A["par"].rearrange("l p c -> p l c")).then_inc(params_in, 16)
            half = KT * SEQ // 2
            for h in range(2):
                sp.dma_start(x[:, h * half:(h + 1) * half], A["x"][:, h * half:(h + 1) * half]).then_inc(x_in[h], 16)
            stream = A["w"]
            for s in range(4):
                sp.dma_start(adaw[:, s, :], A["ada"][s]).then_inc(ada_in[s], 16)

            def refill(n, parity):
                sp.wait_ge(w_lo, n - 1)
                src = stream[n] if isinstance(n, int) else stream[bass.ds(n, 1)].rearrange("a p c -> p (a c)")
                sp.dma_start(raw[:, parity, :], src).then_inc(w_in[parity], 16)

            def ada_refill(u, slot):
                sp.wait_ge(ada_used, u - 3)
                src = A["ada"][u] if isinstance(u, int) else A["ada"][bass.ds(u, 1)].rearrange("a p c -> p (a c)")
                sp.dma_start(adaw[:, slot, :], src).then_inc(ada_in[slot], 16)

            for u in range(4, 2 * KT):
                if u == 2 * KT - 2:
                    for s in range(2):
                        sp.dma_start(raw[:, s, :], stream[s]).then_inc(w_in[s], 16)
                ada_refill(u, u % 4)
            for n in (2, 3):
                refill(n, n % 2)
            for u in range(2 * KT, 2 * KT + 4):
                ada_refill(u, u % 4)
            sp.dma_start(gw[:, :, :], A["gw"][0]).then_inc(gw_in, 16)
            for l in range(DEPTH):
                B = step_base(l)
                for i in range(NPROJ + NOUT):
                    refill(B + i + 4, i % 2)
                    for k in MAC_STEPS[l].get(i, []):
                        u = MAC_FIRST[l] + k + 4
                        if u < DEPTH * NMOD * KT:
                            ada_refill(u, u % 4)
                for g in range(GROUPS):
                    G = B + NPROJ + NOUT + g * GSTEP
                    with sp.Fori(0, 2) as it:
                        for c in range(8):
                            refill(it * 8 + (G + c + 4), c % 2)
                            if l == 0:
                                for kt in UP_MACS.get(c, []):
                                    ada_refill(it * KT + ((NMOD - 1 + 2 * g) * KT + kt + 4), kt % 4)
                    if l + 1 < DEPTH or g + 1 < GROUPS:
                        with sp.Fori(0, KT // 2) as it:
                            for c in range(2):
                                refill(it * 2 + (G + 2 * KT + c + 4), c)
                    else:
                        for j in range(KT - 4):
                            refill(G + 2 * KT + j + 4, j % 2)
            for j in range(KT):
                sp.wait_ge(*x_new(DEPTH - 1, 1, j))
                sp.dma_start(A["out"][:, j * SEQ:(j + 1) * SEQ], xt(j)).then_inc(stored, 16)
            sp.wait_ge(stored, 16 * KT)

        @block.gpsimd
        def _(pool):
            made = 0

            def const(tile, value):
                nonlocal made
                nc.gpsimd.memset(tile, value).then_inc(consts, 1)
                made += 1
                pool.wait_ge(consts, made)
            const(ident[:, :], 0.0)
            const(ones[:, :], 1.0)
            const(eps, EPS)
            const(kd[:, :, 0:CHUNK], 0.0)
            for q4 in range(4):
                const(sign[32 * q4:32 * q4 + 32, :], -1.0 if q4 % 2 == 0 else 1.0)
            nc.gpsimd.affine_select(out=ident[:, :], in_=ident[:, :], compare_op=ALU.not_equal, fill=1.0,
                                    base=0, pattern=[[-1, P]], channel_multiplier=1).then_inc(consts, 1)
            GTT, GTS = nc.gpsimd.tensor_tensor, nc.gpsimd.tensor_scalar
            W = Tally(pool_self)

            def link(ins):
                W.mark(ins)
                pool.wait_ge(pool_self, W.n)

            pool.wait_ge(presq_ready, 1)
            for j in range(1, KT):
                pool.wait_ge(presq_ready, j + 1)
                GTT(ssq, ssq, presq[(j - 1) % 3], ALU.add).then_inc(presq_used, 1)
                pool.wait_ge(presq_used, j)
            pool.wait_ge(sin_ready, 2)
            link(GTS(sinT[:, :], sinT[:, :], sign, 0.0, ALU.mult, ALU.add))
            link(GTT(cosT[:, :], cosT[:, :], cosT[:, :], ALU.mult))
            GTS(cosT[:, :], cosT[:, :], -2.0, 1.0, ALU.mult, ALU.add).then_inc(rope_ready, 1)
            pool.wait_ge(sp_recip, 1)
            lam = par[:, :, COLS["lam"]:COLS["lam"] + LT]
            s1, s2, s3 = sp1[:, :, :], sp2[:, :, :], sp3[:, :, :]
            link(GTT(s2, s2, s1, ALU.mult))
            link(GTT(s1, s2, s2, ALU.mult))
            link(GTS(s3, s1, 1.0 / 17, 1.0 / 15, ALU.mult, ALU.add))
            for k in range(13, 0, -2):
                link(GTT(s3, s3, s1, ALU.mult))
                link(GTS(s3, s3, 1.0 / k, 1.0, ALU.add, ALU.mult))
            link(GTT(s3, s3, s2, ALU.mult))
            link(GTS(s1, lam, -0.5, 0.0, ALU.mult, ALU.max))
            link(GTT(s3, s3, s1, ALU.add))
            link(GTS(spl[:, :, :], s3, 8.0, 0.0, ALU.mult, ALU.add))
            GTS(nspl[:, :, :], s3, -16.0, 0.0, ALU.mult, ALU.add).then_inc(sp_ready, 1)

            def add_to_x(l, k):
                for j in X_POOL:
                    pool.wait_ge(y_scaled, (2 * l + k) * KT + j + 1)
                    GTT(xt(j), xt(j), yt(j), ALU.add).then_inc(x_done, 1)

            def lo_tiles(k0, dst, hi, biased):
                for j in LO_POOL:
                    if biased:
                        pool.wait_ge(pool_hi, biased_before(k0) * len(LO_POOL) + LO_POOL.index(j) + 1)
                    else:
                        pool.wait_ge(hi_ready, k0 + j + 1)
                    GTT(dst[:, j, :], yt(j), hi[:, j, :].bitcast(fp32), ALU.subtract).then_inc(lo_ready2, 1)

            def biased_before(k0):
                k = k0 // KT
                return k - (k + 1) // 3 if k else 0

            lo_tiles(0, hL, hH, True)
            for l in range(DEPTH):
                for j in range(LT):
                    pool.wait_ge(sig_done, l * LT + j + 1)
                    GTT(I[:, j, :], I[:, j, :], xc[:, j, :], ALU.mult).then_inc(gated_ready, 1)
                pool.wait_ge(root_ready, l + 1)
                for j in range(LT):
                    pool.wait_ge(gated_ready, l * LT + j + 1)
                    GTT(I[:, j, :], I[:, j, :], R[:, j, :], ALU.mult).then_inc(drive_ready, 1)
                for t in range(QT - 1):
                    pool.wait_ge(den_ready, l * (QT - 1) + t + 1)
                    sc = scores[t % 2].rearrange("p (s k) -> p s k", s=NQ)
                    GTT(sc, sc, den[t % 2].unsqueeze(2).broadcast_to([P, NQ, P]), ALU.mult).then_inc(p_ready, 1)
                pool.wait_ge(scan_done, (l + 1) * LT)
                pool.wait_ge(gelu_ready, l + 1)
                for j in range(LT):
                    if j == LT - 1:
                        pool.wait_ge(*proj_release(l, NPROJ - 1))
                    GTT(yt(AT + j), yt(AT + j), xc[:, j, :], ALU.mult).then_inc(l_ready, 1)
                lo_tiles(conv_no(l, 0), mL, mH, False)
                add_to_x(l, 0)
                lo_tiles(conv_no(l, 1), hL, hH, True)
                add_to_x(l, 1)
                if l + 1 < DEPTH:
                    lo_tiles(conv_no(l, 2), hL, hH, True)
        NCONST = 9

        @block.scalar
        def _(act):
            S = Tally(act_self)

            def self_wait():
                act.wait_ge(act_self, S.n)

            def split_step(n, s, first=False):
                if not first:
                    act.wait_ge(chunk_done, n - 1)
                act.wait_ge(w_in[s], (n - s) * 8 + 16)
                nc.scalar.activation(wH[:, s, :], raw[:, s, :], ACT.Copy).then_inc(w_hi, 1)

            def fetch_sqrt():
                nc.scalar.activation(tiny[:, 60:61], eps, ACT.Sqrt)

            def sd_step(m, dim, groups=1):
                act.wait_ge(cols_ready, COL_NORMS.index(m) + 1)
                nc.scalar.activation(sd8[:, 0:groups * QT], cols_bank(m)[:, 0:groups * QT], ACT.Sqrt, bias=eps,
                                     scale=1.0 / dim).then_inc(sd_ready, 1)

            def squares_of(m0, j, src, wait_sem, wait_value, own=False):
                if not own:
                    act.wait_ge(wait_sem, wait_value)
                if j >= 2:
                    act.wait_ge(sq_used, m0 + j - 1)
                dst = ssq if j == 0 else sqb[j % 2]
                nc.scalar.activation(dst, src, ACT.Square).then_inc(sq_ready, 1)

            def x_norm(l, k):
                i = X_NORMS.index(norm_no(l, k + 1))
                for j in range(KT):
                    act.wait_ge(*x_new(l, k // 2, j))
                    if j >= 4:
                        act.wait_ge(xsq_used, i * (KT - 1) + j - 3)
                    nc.scalar.activation(xsqb[j % 4], xt(j), ACT.Square).then_inc(xsq_ready, 1)
                act.wait_ge(xsum_ready, i + 1)
                nc.scalar.activation(ssq[0:1, :], bank(XSUM)[0:1, :], ACT.Sqrt, bias=eps[0:1, :],
                                     scale=1.0 / D).then_inc(sd_row, 1)

            def hi_tiles(k0, dst, bias):
                for j in range(KT):
                    act.wait_ge(tmp_ready, k0 + j + 1)
                    if bias is None:
                        nc.scalar.activation(dst[:, j, :], yt(j), ACT.Copy).then_inc(hi_ready, 1)
                    else:
                        nc.scalar.activation(dst[:, j, :], yt(j), ACT.Identity,
                                             bias=bias[:, j:j + 1], scale=1.0).then_inc(hi_ready, 1)
                        if j in LO_POOL:
                            nc.scalar.activation(yt(j), yt(j), ACT.Identity,
                                                 bias=bias[:, j:j + 1], scale=1.0).then_inc(pool_hi, 1)

            act.wait_ge(early_in, 48)
            nc.scalar.activation(ctmp, craw, ACT.Exp, scale=-1.0).then_inc(c_exp, 1)
            act.wait_ge(params_in, 16)
            lam = par[:, :, COLS["lam"]:COLS["lam"] + LT]
            S.mark(nc.scalar.activation(sp1[:, :, :], lam, ACT.Abs))
            self_wait()
            nc.scalar.activation(sp2[:, :, :], sp1[:, :, :], ACT.Exp, scale=-1.0).then_inc(sp_exp, 1)
            for j in range(KT):
                if j % (KT // 2) == 0:
                    act.wait_ge(x_in[j // (KT // 2)], 16)
                if j >= 4:
                    act.wait_ge(presq_used, j - 3)
                nc.scalar.activation(presq[(j - 1) % 3] if j else ssq, xt(j), ACT.Square).then_inc(presq_ready, 1)
                if j == 2:
                    act.wait_ge(ang_ready, 1)
                    nc.scalar.activation(sinT[:, :], R[:, 0, :], ACT.Sin).then_inc(sin_ready, 1)
                    nc.scalar.activation(cosT[:, :], R[:, 0, :], ACT.Sin, scale=0.5).then_inc(sin_ready, 1)
            sd_step(0, D)
            split_step(0, 0, True)
            split_step(1, 1, True)
            act.wait_ge(mod_done, 2)
            hi_tiles(0, hH, mod[:, 0, :])

            for l in range(DEPTH):
                B = step_base(l)
                par_l = par[:, l, :]
                for i, kind in enumerate(PROJ):
                    n = B + i
                    if i < NPROJ - 1:
                        split_step(n + 2, n % 2)
                    acc = bank(i % 2)
                    first_g = NPROJ - LT
                    act.wait_ge(chunk_done, n + 1)
                    if kind == "x":
                        nc.scalar.activation(xc[:, i, :], acc, ACT.Identity, bias=pcol(l, "lcb", i),
                                             scale=pcol(l, "lcw", (CONVW - 1) * LT + i)).then_inc(x_base, 1)
                    elif kind in "kq":
                        if kind == "q":
                            act.wait_ge(*proj_release(l, i - 1))
                        for q4 in range(4):
                            o = q4 ^ 1
                            last = nc.scalar.activation(scr[32 * q4:32 * q4 + 32, 0:SEQ],
                                                        acc[32 * o:32 * o + 32, :], ACT.Copy)
                        last.then_inc(swap_ready, 1)
                    elif kind == "v":
                        act.wait_ge(v_pad, l + 1)
                        nc.scalar.activation(vT[:, CHUNK:], acc, ACT.Copy).then_inc(acc_act, 1)
                    else:
                        j = i - (NPROJ - LT)
                        act.wait_ge(gated_ready, l * LT + j + 1)
                        if j < LT - 1:
                            nc.scalar.activation(xc[:, j, :], acc, ACT.Copy).then_inc(acc_act, 1)
                        else:
                            nc.scalar.activation(xc[:, j, :], acc, ACT.Gelu_apprx_tanh).then_inc(acc_act, 1)
                    if 1 <= i <= LT:
                        j = i - 1
                        act.wait_ge(gate_mm, l * LT + j + 1)
                        b = 2 + 2 * (j % 2)
                        S.mark(nc.scalar.activation(R[:, j, :], bank(b), ACT.Sigmoid, bias=pcol(l, "ba", j)))
                        nc.scalar.activation(I[:, j, :], bank(b + 1), ACT.Sigmoid,
                                             bias=pcol(l, "bx", j)).then_inc(sig_done, 1)
                    if l == 0 and i == LT + 1:
                        act.wait_ge(sp_ready, 1)
                    if LT < i <= 2 * LT:
                        for j in [i - LT - 1]:
                            self_wait()
                            S.mark(nc.scalar.activation(Adec[:, j, :], R[:, j, :], ACT.Exp,
                                                        scale=nspl[:, l, j:j + 1]))
                            self_wait()
                            nc.scalar.activation(R[:, j, :], R[:, j, :], ACT.Tanh,
                                                 scale=spl[:, l, j:j + 1]).then_inc(aT_ready, 1)
                    if i == 2 * LT:
                        act.wait_ge(b2_ready, (l + 1) * LT)
                        nc.scalar.activation(Rf, Rf, ACT.Sqrt).then_inc(root_ready, 1)
                    if i == first_g:
                        act.wait_ge(vw_mm, l + 1)
                        nc.scalar.activation(vw[:, :, :].rearrange("p a b -> p (a b)"), bank(4, 2),
                                             ACT.Copy).then_inc(vw_ready, 1)

                    def exps(t):
                        act.wait_ge(s_sub, l * QT + t + 1)
                        nc.scalar.activation(es[t % 2], es[t % 2], ACT.Exp)
                        nc.scalar.activation(scores[t % 2], scores[t % 2], ACT.Exp).then_inc(s_exp, 1)

                    def copy_pt(t):
                        act.wait_ge(pt_mm, l * QT + t + 1)
                        if t >= 2:
                            act.wait_ge(o_mm, l * QT + t - 1)
                        nc.scalar.activation(probsT[t % 2], bank(4, 2), ACT.Copy).then_inc(pt_copied, 1)

                    def copy_out(t):
                        act.wait_ge(o_mm, l * QT + t + 1)
                        o4 = bank(6).rearrange("p (j q) -> p j q", j=AT)
                        dst = y[:, 0:AT * SEQ].rearrange("p (j q) -> p j q", j=AT)[:, :, t * P:(t + 1) * P]
                        nc.scalar.activation(dst, o4, ACT.Copy)
                        if t >= 1:
                            act.wait_ge(osq_ready, l * QT + t)
                        nc.scalar.activation(sq[:, :], bank(6), ACT.Square).then_inc(o_copied, 1)

                    if i == first_g - 1:
                        exps(0)
                    if i == first_g:
                        exps(1)
                    if i == first_g + 1:
                        copy_pt(0); exps(2)
                    if i == first_g + 2:
                        copy_out(0); copy_pt(1); exps(3)
                        xcf = xc[:, 0:LT - 1, :].rearrange("p a b -> p (a b)")
                        act.wait_ge(acc_act, proj_release(l, i)[1])
                        nc.scalar.activation(xcf, xcf, ACT.Gelu_apprx_tanh).then_inc(gelu_ready, 1)
                    if i == first_g + 3:
                        copy_out(1); copy_pt(2)
                        split_step(n + 2, n % 2)
                        fetch_sqrt()
                        copy_out(2)
                        for j in range(LT):
                            act.wait_ge(l_ready, l * LT + j + 1)
                            nc.scalar.activation(I[:, j, :], yt(AT + j), ACT.Square).then_inc(lsq_ready, 1)
                        copy_out(3)
                sd_step(norm_no(l, 0), D_ATTN, 2)
                hi_tiles(conv_no(l, 0), mH, None)
                for j in range(NOUT):
                    n = B + NPROJ + j
                    act.wait_ge(chunk_done, n + 1)
                    if j == 0:
                        act.wait_ge(*lo_part(conv_no(l, 0), LO_DVE[-1]))
                        act.wait_ge(*lo_part(conv_no(l, 0), LO_POOL[-1]))
                    acc = bank(j % 2)
                    if j >= 2:
                        act.wait_ge(sq_used, sq_no(l, 0) + j - 1)
                    dst = ssq if j == 0 else sqb[j % 2]
                    nc.scalar.activation(dst, acc, ACT.Square).then_inc(sq_ready, 1)
                    nc.scalar.activation(yt(j), acc, ACT.Copy).then_inc(out_copied, 1)
                    split_step(n + 2, n % 2)
                sd_step(norm_no(l, 1), D)
                x_norm(l, 1)
                hi_tiles(conv_no(l, 1), hH, mod[:, l * NMOD + 3, :])
                if l + 1 < DEPTH:
                    act.dma_start(gw[:, :, :], A["gw"][l + 1]).then_inc(gw_in, 16)

                for g in range(GROUPS):
                    G = B + NPROJ + NOUT + g * GSTEP
                    U = l * 2 * PAIRS + g * 2 * KT
                    Q = l * PAIRS + g * KT
                    with act.Fori(0, 2) as it:
                        for c in range(8):
                            n = it * 8 + G + c
                            u = it * 8 + U + c
                            pr = it * 4 + Q + c // 2
                            if c % 2:
                                act.wait_ge(f_taps, u + 4)
                                nc.scalar.activation(I[:, (c // 2) % 2, :], R[:, (c - 1) % 4, :],
                                                     ACT.Gelu_apprx_tanh).then_inc(f_gelu, 1)
                            act.wait_ge(chunk_done, n + 1)
                            col = it * 4 + (g * KT + c // 2 + (c % 2) * PAIRS)
                            nc.scalar.activation(
                                R[:, c % 4, :], bank(c % 4), ACT.Identity,
                                bias=par_l[:, bass.ds(col + COLS["fcb"], 1)],
                                scale=par_l[:, bass.ds(col + (COLS["fcw"] + 2 * 2 * PAIRS), 1)]).then_inc(f_base, 1)
                            split_step(n + 2, c % 2)
                            if c % 2:
                                act.wait_ge(f_mul, pr + 1)
                                nc.scalar.activation(mH[:, bass.ds(it * 4 + c // 2, 1), :].rearrange("p a b -> p (a b)"),
                                                     I[:, 2 + (c // 2) % 2, :], ACT.Copy).then_inc(act_hi, 1)
                    last_group = g == GROUPS - 1
                    V = G + 2 * KT
                    if last_group:
                        fetch_sqrt()
                    if not last_group:
                        with act.Fori(0, KT // 2) as it:
                            for c in range(2):
                                split_step(it * 2 + (V + c + 2), c % 2)
                    else:
                        for j in range(KT):
                            squares_of(sq_no(l, 1), j, yt(j), dn_read, l * KT * GROUPS + g * KT + j + 1 + 2)
                            if V + j + 2 < DEPTH * NCH:
                                split_step(V + j + 2, j % 2)
                sd_step(norm_no(l, 3), D)
                if l + 1 < DEPTH:
                    x_norm(l, 3)
                    hi_tiles(conv_no(l, 2), hH, mod[:, (l + 1) * NMOD, :])

        @block.vector
        def _(dve):
            V = Tally(dve_self)
            TT, TS, STT = nc.vector.tensor_tensor, nc.vector.tensor_scalar, nc.vector.scalar_tensor_tensor

            def self_wait():
                dve.wait_ge(dve_self, V.n)

            def link(ins):
                V.mark(ins)
                self_wait()

            def lo_chunk(n, parity):
                dve.wait_ge(w_hi, n + 1)
                TT(wL[:, parity, :], raw[:, parity, :], wH[:, parity, :].bitcast(fp32),
                   ALU.subtract).then_inc(w_lo, 1)

            def mac_unit(seg, kt):
                u, slot = seg * KT + kt, kt % 4
                if kt == 0 and not (isinstance(seg, int) and seg == 0):
                    dve.wait_ge(mod_cols, seg + 0)
                dve.wait_ge(ada_in[slot], (seg * 2 + kt // 4 + 1) * 16)
                if kt == 0:
                    ins = TS(macc[:, :], adaw[:, slot, :], csil[:, kt:kt + 1], None, ALU.mult)
                else:
                    ins = STT(out=macc[:, :], in0=adaw[:, slot, :], scalar=csil[:, kt:kt + 1], in1=macc[:, :],
                              op0=ALU.mult, op1=ALU.add)
                ins.then_inc(ada_used, 1)
                dve.wait_ge(ada_used, u + 1)
                if kt == KT - 1:
                    dve.sem_inc(macc_ready, 1)

            def mod_store(seg, bcol):
                dve.wait_ge(mod_cols, seg + 1)
                V.mark(nc.vector.tensor_reduce(msum[:, :], bank(6, 2).rearrange("p (j q) -> p j q", j=KT),
                                               AX.X, ALU.add))
                self_wait()
                out = mod[:, seg, :] if isinstance(seg, int) else mod[:, bass.ds(seg, 1), :].rearrange("p a b -> p (a b)")
                TT(out, msum[:, :], bcol, ALU.add).then_inc(mod_done, 1)
                dve.wait_ge(mod_done, seg + 1)

            def mod_bias(seg):
                l, s = divmod(seg, NMOD)
                c = COLS["ada_b"] + s * KT
                return par[:, l, c:c + KT]

            def factors(l, which):
                seg, gain = [(1, "mix_pre"), (2, "mix_post"), (4, "ffn_pre"), (5, "ffn_post")][which]
                g = par[:, l, COLS[gain]:COLS[gain] + KT]
                m = mod[:, l * NMOD + seg, :]
                if which % 2 == 0:
                    link(STT(out=fac[:, l, which, :], in0=m, scalar=1.0, in1=g, op0=ALU.add, op1=ALU.mult))
                else:
                    link(TT(fac[:, l, which, :], m, g, ALU.mult))

            def make_rs(m, groups=1):
                if m in X_NORMS:
                    dve.wait_ge(sd_cols, X_NORMS.index(m) + 1)
                    nc.vector.reciprocal(rs8[:, 0:QT], bank(7)[:, 0:QT]).then_inc(rs_ready, 1)
                else:
                    dve.wait_ge(sd_ready, COL_NORMS.index(m) + 1)
                    n = groups * QT
                    nc.vector.reciprocal(rs8[:, 0:n], sd8[:, 0:n]).then_inc(rs_ready, 1)

            def add_square(m0, j):
                dve.wait_ge(sq_ready, m0 + j + 1)
                if j > 0:
                    TT(ssq, ssq, sqb[j % 2], ALU.add).then_inc(sq_used, 1)
                else:
                    dve.sem_inc(sq_used, 1)
                dve.wait_ge(sq_used, m0 + j + 1)
                if j == KT - 1:
                    dve.sem_inc(ssq_ready, 1)

            def split_tiles(k0, src, gains, rbs, dst, bias, x_of=None):
                def tmp(j):
                    if x_of:
                        dve.wait_ge(*x_new(*x_of, j))
                    STT(out=yt(j), in0=src(j), scalar=gains(j), in1=rbs(j), op0=ALU.mult,
                        op1=ALU.mult).then_inc(tmp_ready, 1)
                tmp(0)
                for j in range(KT):
                    if j + 1 < KT:
                        tmp(j + 1)
                    if j in LO_POOL:
                        continue
                    dve.wait_ge(hi_ready, k0 + j + 1)
                    if bias is None:
                        TT(dst[:, j, :], yt(j), hi_of(dst)[:, j, :], ALU.subtract).then_inc(lo_ready, 1)
                    else:
                        STT(out=dst[:, j, :], in0=yt(j), scalar=bias[:, j:j + 1],
                            in1=hi_of(dst)[:, j, :], op0=ALU.add, op1=ALU.subtract).then_inc(lo_ready, 1)

            def hi_of(dst):
                return (hH if dst is hL else mH)[:, :, :].bitcast(fp32)

            dve.sem_inc(f_taps, 4)
            dve.sem_inc(dn_read, 2)
            dve.wait_ge(early_in, 48)
            ang, turns = R[:, 0, :], R[:, 1, :]
            link(nc.vector.tensor_copy(R[:, 2, :], Adec[:, 0, :].bitcast(i32)))
            link(TS(ang, R[:, 2, :], freq, None, ALU.mult))
            for unit in (COARSE, 1.0):
                link(TS(turns, ang, 1.0 / (TWO_PI * unit), ROUND_MAGIC, ALU.mult, ALU.add))
                link(TS(turns, turns, ROUND_MAGIC, None, ALU.subtract))
                for part in PI_PARTS:
                    link(STT(out=ang, in0=turns, scalar=-part * unit, in1=ang, op0=ALU.mult, op1=ALU.add))
            PI = 3.1415925
            TS(ang, ang, PI, -PI, ALU.min, ALU.max).then_inc(ang_ready, 1)
            dve.wait_ge(c_exp, 1)
            link(TS(ctmp, ctmp, 1.0, None, ALU.add))
            link(nc.vector.reciprocal(ctmp, ctmp))
            link(TT(csil, craw, ctmp, ALU.mult))
            dve.wait_ge(sp_exp, 1)
            link(TS(sp1[:, :, :], sp2[:, :, :], 2.0, None, ALU.add))
            nc.vector.reciprocal(sp1[:, :, :], sp1[:, :, :]).then_inc(sp_recip, 1)
            for kt in range(KT):
                mac_unit(0, kt)
            dve.wait_ge(params_in, 16)
            for kt in range(KT):
                mac_unit(1, kt)
                if kt == 0:
                    mod_store(0, mod_bias(0))
                if kt == KT // 2:
                    make_rs(0)
                if kt == KT - 3:
                    lo_chunk(0, 0)
                    lo_chunk(1, 1)
            mod_store(1, mod_bias(1))
            factors(0, 0)
            dve.wait_ge(rb_ready, 1)
            split_tiles(0, xt, lambda j: fac[:, 0, 0, j:j + 1], lambda j: bank(2), hL, mod[:, 0, :])

            for l in range(DEPTH):
                B = step_base(l)
                par_l = par[:, l, :]

                def extra(i):
                    for k in MAC_STEPS[l].get(i, []):
                        seg, kt = divmod(MAC_FIRST[l] + k, KT)
                        mac_unit(seg, kt)
                    if i in MOD_AT[l]:
                        seg = MOD_AT[l][i]
                        mod_store(seg, mod_bias(seg))

                def softmax(t):
                    sc = scores[t % 2].rearrange("p (s k) -> p s k", s=NQ)
                    m8, e8 = mx[t % 2], es[t % 2]
                    bc = lambda v: v.unsqueeze(2).broadcast_to([P, NQ, P])
                    sink = par_l[:, COLS["sink"]:COLS["sink"] + NQ]
                    dve.wait_ge(s_mm, l * QT + t + 1)
                    raw_s = bank(2, 2).rearrange("p (s k) -> p s k", s=NQ)
                    if t == 0:
                        link(nc.vector.memset(raw_s[0:CHUNK, :, 0:CHUNK], MASK))
                    link(nc.vector.tensor_reduce(m8, raw_s, AX.X, ALU.max))
                    link(STT(out=m8, in0=m8, scalar=HD ** -0.5, in1=sink, op0=ALU.mult, op1=ALU.max))
                    TT(e8, sink, m8, ALU.subtract)
                    if t == 1:
                        dve.wait_ge(drive_ready, (l + 1) * LT)
                    if t >= 2:
                        dve.wait_ge(pt_mm, l * QT + t - 1)
                    STT(out=sc, in0=raw_s, scalar=HD ** -0.5, in1=bc(m8), op0=ALU.mult,
                        op1=ALU.subtract).then_inc(s_sub, 1)

                def normalise(t):
                    sc = scores[t % 2].rearrange("p (s k) -> p s k", s=NQ)
                    e8, d8 = es[t % 2], den[t % 2]
                    bc = lambda v: v.unsqueeze(2).broadcast_to([P, NQ, P])
                    dve.wait_ge(s_exp, l * QT + t + 1)
                    link(nc.vector.tensor_reduce(d8, sc, AX.X, ALU.add))
                    link(TT(d8, d8, e8, ALU.add))
                    if t < QT - 1:
                        nc.vector.reciprocal(d8, d8).then_inc(den_ready, 1)
                    else:
                        link(nc.vector.reciprocal(d8, d8))
                        TT(sc, sc, bc(d8), ALU.mult).then_inc(p_last, 1)

                def out_squares(t):
                    dve.wait_ge(o_copied, l * QT + t + 1)
                    nc.vector.tensor_reduce(ssq[:, t * P:(t + 1) * P],
                                            sq[:, :].rearrange("p (j q) -> p q j", j=AT),
                                            AX.X, ALU.add).then_inc(osq_ready, 1)

                for i, kind in enumerate(PROJ):
                    n = B + i
                    if i == NPROJ - 1:
                        out_squares(0)
                        out_squares(1)
                    lo_chunk(n + 2, n % 2)
                    acc = bank(i % 2)
                    if kind == "x":
                        dve.wait_ge(x_base, l * LT + i + 1)
                        for k in range(CONVW - 2, -1, -1):
                            back = CONVW - 1 - k
                            ins = STT(out=xc[:, i, back:], in0=acc[:, 0:SEQ - back],
                                      scalar=pcol(l, "lcw", k * LT + i), in1=xc[:, i, back:],
                                      op0=ALU.mult, op1=ALU.add)
                            if k:
                                link(ins)
                        ins.then_inc(acc_dve, 1)
                    elif kind in "kq":
                        j = i - LT
                        if l == 0 and kind == "k":
                            dve.wait_ge(rope_ready, 1)
                        dve.wait_ge(swap_ready, l * (AT + 1) + j + 1)
                        t1, t2 = scr[:, SEQ:2 * SEQ], scr[:, 0:SEQ]
                        V.mark(TT(t1, acc, cosT[:, :], ALU.mult))
                        link(TT(t2, t2, sinT[:, :], ALU.mult))
                        if kind == "q":
                            TT(yt(i - LT - 1), t1, t2, ALU.add).then_inc(acc_dve, 1)
                        else:
                            V.mark(TT(kd[0:HD, 0, CHUNK:], t1[0:HD], t2[0:HD], ALU.add))
                            link(TT(kd[HD:P, 1, CHUNK:], t1[HD:P], t2[HD:P], ALU.add))
                            nc.vector.tensor_copy(kd[HD:P, 0, CHUNK:], kd[0:HD, 0, CHUNK:])
                            nc.vector.tensor_copy(kd[0:HD, 1, CHUNK:], kd[HD:P, 1, CHUNK:]).then_inc(acc_dve, 1)
                            nc.vector.memset(vT[:, 0:CHUNK], 0.0).then_inc(v_pad, 1)
                    if LT < i <= 2 * LT:
                        for j in [i - LT - 1]:
                            dve.wait_ge(aT_ready, l * LT + j + 1)
                            link(STT(out=R[:, j, :], in0=Adec[:, j, :], scalar=1.0, in1=R[:, j, :],
                                     op0=ALU.add, op1=ALU.mult))
                            link(TS(Adec[:, j, :], R[:, j, :], -1.0, 1.0, ALU.mult, ALU.add))
                            STT(out=R[:, j, :], in0=Adec[:, j, :], scalar=1.0, in1=R[:, j, :],
                                op0=ALU.add, op1=ALU.mult).then_inc(b2_ready, 1)
                    t = i - (NPROJ - LT - 1)
                    if 0 <= t < QT:
                        softmax(t)
                    if i == 2 * LT + 2:
                        for j in range(LT):
                            dve.wait_ge(drive_ready, l * LT + j + 1)
                            nc.vector.tensor_tensor_scan(yt(AT + j), Adec[:, j, :], I[:, j, :], 0.0,
                                                         ALU.mult, ALU.add).then_inc(scan_done, 1)
                    extra(i)
                    if 0 <= t < QT:
                        normalise(t)
                dve.wait_ge(pt_mm, (l + 1) * QT)
                dve.wait_ge(o_mm, l * QT + QT - 2)
                nc.vector.tensor_copy(probsT[(QT - 1) % 2], bank(4, 2)).then_inc(pt_last, 1)
                out_squares(2)
                dve.wait_ge(lsq_ready, l * LT + 2)
                link(TT(I[:, 0, :], I[:, 0, :], I[:, 1, :], ALU.add))
                for j in range(2, LT):
                    dve.wait_ge(lsq_ready, l * LT + j + 1)
                    link(TT(I[:, 0, :], I[:, 0, :], I[:, j, :], ALU.add))
                dve.sem_inc(lru_summed, 1)
                out_squares(QT - 1)
                dve.wait_ge(osq_ready, (l + 1) * QT)
                dve.sem_inc(ssq_ready, 1)
                make_rs(norm_no(l, 0), 2)
                dve.wait_ge(rb_ready, norm_no(l, 0) + 1)
                split_tiles(conv_no(l, 0), yt,
                            lambda j: pcol(l, "g_attn", j) if j < AT else pcol(l, "g_lru", j - AT),
                            lambda j: bank(2 if j < AT else 3), mL, None)
                factors(l, 1)
                for j in range(NOUT):
                    n = B + NPROJ + j
                    add_square(sq_no(l, 0), j)
                    if j == NOUT - 1:
                        make_rs(norm_no(l, 1))
                    lo_chunk(n + 2, n % 2)
                    extra(NPROJ + j)

                def scale_y(which, k):
                    rb = bank(RB_BANK[k])
                    for j in range(KT):
                        STT(out=yt(j), in0=yt(j), scalar=fac[:, l, which, j:j + 1], in1=rb,
                            op0=ALU.mult, op1=ALU.mult).then_inc(y_scaled, 1)
                        if j in X_DVE:
                            dve.wait_ge(y_scaled, (2 * l + k // 2) * KT + j + 1)
                            TT(xt(j), xt(j), yt(j), ALU.add).then_inc(x_done2, 1)

                dve.wait_ge(rb_ready, norm_no(l, 1) + 1)
                dve.wait_ge(out_copied, (l + 1) * NOUT)
                scale_y(1, 1)
                factors(l, 2)
                make_rs(norm_no(l, 2))
                dve.wait_ge(rb_ready, norm_no(l, 2) + 1)
                split_tiles(conv_no(l, 1), xt, lambda j: fac[:, l, 2, j:j + 1], lambda j: bank(RB_BANK[2]),
                            hL, mod[:, l * NMOD + 3, :], (l, 0))

                for g in range(GROUPS):
                    G = B + NPROJ + NOUT + g * GSTEP
                    U = l * 2 * PAIRS + g * 2 * KT
                    Q = l * PAIRS + g * KT
                    start, marks = V.n, V.marks
                    PER = 8 + (l == 0)
                    with dve.Fori(0, 2) as it:
                        V.n = it * PER + start
                        for c in range(8):
                            n = it * 8 + G + c
                            u = it * 8 + U + c
                            dve.wait_ge(f_base, u + 1)
                            col = it * 4 + (g * KT + c // 2 + (c % 2) * PAIRS)
                            buf, acc = R[:, c % 4, :], bank(c % 4)
                            link(STT(out=buf[:, 1:], in0=acc[:, 0:SEQ - 1],
                                     scalar=par_l[:, bass.ds(col + (COLS["fcw"] + 2 * PAIRS), 1)],
                                     in1=buf[:, 1:], op0=ALU.mult, op1=ALU.add))
                            STT(out=buf[:, 2:], in0=acc[:, 0:SEQ - 2],
                                scalar=par_l[:, bass.ds(col + COLS["fcw"], 1)],
                                in1=buf[:, 2:], op0=ALU.mult, op1=ALU.add).then_inc(f_taps, 1)
                            if c % 2:
                                pr, p = it * 4 + Q + c // 2, c // 2
                                dve.wait_ge(f_gelu, pr + 1)
                                dve.wait_ge(f_taps, u + 5)
                                TT(I[:, 2 + p % 2, :], I[:, p % 2, :], buf, ALU.mult).then_inc(f_mul, 1)
                            lo_chunk(n + 2, c % 2)
                            if c % 2:
                                dve.wait_ge(act_hi, pr + 1)
                                at = bass.ds(it * 4 + p, 1)
                                TT(mL[:, at, :].rearrange("p a b -> p (a b)"), I[:, 2 + p % 2, :],
                                   mH[:, at, :].rearrange("p a b -> p (a b)").bitcast(fp32),
                                   ALU.subtract).then_inc(act_lo, 1)
                            if l == 0:
                                for kt in UP_MACS.get(c, []):
                                    mac_unit(it + (NMOD - 1 + 2 * g), kt)
                        if l == 0:
                            seg = it + (NMOD - 1 + 2 * g)
                            bl, bs = divmod(NMOD - 1 + 2 * g, NMOD)
                            if g == 0:
                                bcol = par[:, :, :].rearrange("p l c -> p (l c)")[
                                    :, bass.ds(it * (NPAR - (NMOD - 1) * KT) + (COLS["ada_b"] + (NMOD - 1) * KT), KT)]
                            else:
                                bcol = par[:, bl, :][:, bass.ds(it * KT + (COLS["ada_b"] + bs * KT), KT)]
                            mod_store(seg, bcol)
                    assert V.marks - marks == PER, V.marks - marks
                    V.n = start + 2 * PER
                    VD = G + 2 * KT

                    def down(n, j, c, square=False):
                        dve.wait_ge(chunk_done, n + 1)
                        acc = bank(4 + c)
                        out = yt(j) if isinstance(j, int) else y[:, :].rearrange("p (j q) -> p j q", j=KT)[
                            :, bass.ds(j, 1), :].rearrange("p a b -> p (a b)")
                        if g == 0:
                            nc.vector.tensor_copy(out, acc).then_inc(dn_read, 1)
                        else:
                            TT(out, acc, out, ALU.add).then_inc(dn_read, 1)
                        if square:
                            add_square(sq_no(l, 1), j)
                        if not (isinstance(n, int) and n + 2 >= DEPTH * NCH):
                            lo_chunk(n + 2, c)

                    if g < GROUPS - 1:
                        with dve.Fori(0, KT // 2) as it:
                            for c in range(2):
                                down(it * 2 + (VD + c), it * 2 + c, c)
                    else:
                        for j in range(KT):
                            down(VD + j, j, j % 2, True)
                factors(l, 3)
                make_rs(norm_no(l, 3))
                dve.wait_ge(rb_ready, norm_no(l, 3) + 1)
                scale_y(3, 3)
                if l + 1 < DEPTH:
                    factors(l + 1, 0)
                    make_rs(norm_no(l, 4))
                    dve.wait_ge(rb_ready, norm_no(l, 4) + 1)
                    split_tiles(conv_no(l, 2), xt, lambda j: fac[:, l + 1, 0, j:j + 1],
                                lambda j: bank(RB_BANK[4]), hL, mod[:, (l + 1) * NMOD, :], (l, 1))

        @block.tensor
        def _(pe):
            def mm(out, a, b, start, stop, **kw):
                return nc.tensor.matmul(out, a, b, start=start, stop=stop, **kw)

            def tile_products(acc, slot, hi_, lo_, ready):
                for kt in range(KT):
                    a, al = wH[:, slot, kt * P:(kt + 1) * P], wL[:, slot, kt * P:(kt + 1) * P]
                    if ready:
                        hi_sem, hi_value, lo_sem, lo_value = ready(kt)
                        pe.wait_ge(hi_sem, hi_value)
                        mm(acc, a, hi_[:, kt, :], kt == 0, False)
                        mm(acc, al, hi_[:, kt, :], False, False)
                        pe.wait_ge(lo_sem, lo_value)
                        last = mm(acc, a, lo_[:, kt, :], False, kt == KT - 1)
                        continue
                    mm(acc, a, hi_[:, kt, :], kt == 0, False)
                    mm(acc, a, lo_[:, kt, :], False, False)
                    last = mm(acc, al, hi_[:, kt, :], False, kt == KT - 1)
                last.then_inc(chunk_done, 1)

            def norm_cols(m, mods, lru=None):
                if mods:
                    pe.wait_ge(mod_done, mods)
                def cols(g, src):
                    for t in range(QT):
                        last = mm(cols_bank(m)[:, g * QT + t:g * QT + t + 1], src[:, t * P:(t + 1) * P],
                                  ones[:, 0:1], True, True)
                    return last
                if lru is not None:
                    keep_clock(8, bank(7)[:, P:2 * P])
                    pe.wait_ge(lru_summed, lru + 1)
                    cols(1, I[:, 0, :])
                if m == 0:
                    pe.wait_ge(presq_used, KT - 1)
                else:
                    pe.wait_ge(ssq_ready, COL_NORMS.index(m))
                cols(0, ssq).then_inc(cols_ready, 1)

            def keep_clock(n, out):
                for _ in range(n):
                    mm(out, ident[:, :], ident[:, :], True, True)

            def x_sum(m, mods):
                i = X_NORMS.index(m)
                keep_clock(8, bank(3)[:, 0:P])
                for j in range(KT):
                    pe.wait_ge(xsq_ready, i * KT + j + 1)
                    ins = mm(bank(XSUM), ones[:, :], xsqb[j % 4], j == 0, j == KT - 1)
                    ins.then_inc(xsq_used if j < KT - 1 else xsum_ready, 1)
                pe.wait_ge(sd_row, i + 1)
                pe.wait_ge(mod_done, mods)
                for t in range(QT):
                    last = mm(bank(7)[:, t:t + 1], ssq[0:1, t * P:(t + 1) * P], ones[0:1, 0:1], True, True)
                last.then_inc(sd_cols, 1)

            def norm_spread(m, b, groups=1):
                pe.wait_ge(rs_ready, m + 1)
                for g in range(groups):
                    for t in range(QT):
                        last = mm(bank(b + g)[:, t * P:(t + 1) * P],
                                  rs8[:, g * QT + t:g * QT + t + 1].broadcast_to([P, P]), ident[:, :], True, True)
                last.then_inc(rb_ready, 1)

            def mod_sum(seg, norms):
                pe.wait_ge(macc_ready, seg + 1)
                if norms:
                    pe.wait_ge(rs_ready, norms)
                if not (isinstance(seg, int) and seg == 0):
                    pe.wait_ge(mod_done, seg + 0)
                for j in range(KT):
                    last = nc.tensor.transpose(bank(6, 2)[:, j * P:(j + 1) * P], macc[:, j * P:(j + 1) * P],
                                               ident[:, :])
                last.then_inc(mod_cols, 1)

            pe.wait_ge(consts, NCONST)
            mod_sum(0, 0)
            norm_cols(0, 1)
            norm_spread(0, 2)
            mod_sum(1, 1)

            for l in range(DEPTH):
                B = step_base(l)

                def gates(j):
                    rel, val = proj_release(l, j)
                    pe.wait_ge(rel, val)
                    if j >= 2:
                        pe.wait_ge(sig_done, l * LT + j - 1)
                    if j == 0:
                        pe.wait_ge(gw_in, 16 * (l + 1))
                    b = 2 + 2 * (j % 2)
                    mm(bank(b), gw[:, j, :], xc[:, j, :], True, True)
                    mm(bank(b + 1), gw[:, LT + j, :], xc[:, j, :], True, True).then_inc(gate_mm, 1)

                def values():
                    pe.wait_ge(*proj_release(l, NPROJ - LT - 1))
                    pe.wait_ge(sig_done, (l + 1) * LT)
                    for w in range(SEQ // CHUNK):
                        last = nc.tensor.transpose(bank(4, 2)[:, w * P:(w + 1) * P],
                                                   vT[:, w * CHUNK:w * CHUNK + P], ident[:, :])
                    last.then_inc(vw_mm, 1)

                def scores_mm(t):
                    if t == 0:
                        rel, val = proj_release(l, NPROJ - LT - 2)
                        pe.wait_ge(rel, val)
                    else:
                        pe.wait_ge(s_sub, l * QT + t)
                    for s in range(NQ):
                        h = SLOTS[s]
                        at = HD * (h % 2)
                        for half in range(2):
                            w = (2 * t + half) * CHUNK
                            last = mm(bank(2, 2)[half * CHUNK:(half + 1) * CHUNK, s * P:(s + 1) * P],
                                      yt(h // 2)[at:at + HD, w:w + CHUNK],
                                      kd[at:at + HD, h // (NQ // NKV), w:w + P], True, True)
                    last.then_inc(s_mm, 1)

                def probs_transposed(t):
                    if t < QT - 1:
                        pe.wait_ge(p_ready, l * (QT - 1) + t + 1)
                    else:
                        pe.wait_ge(p_last, l + 1)
                    if t == 0:
                        pe.wait_ge(vw_ready, l + 1)
                    else:
                        pe.wait_ge(pt_copied, l * (QT - 1) + t)
                    for s in range(NQ):
                        last = nc.tensor.transpose(bank(4, 2)[:, s * P:(s + 1) * P],
                                                   scores[t % 2][:, s * P:(s + 1) * P], ident[:, :])
                    last.then_inc(pt_mm, 1)

                def outputs_mm(t):
                    if t < QT - 1:
                        pe.wait_ge(pt_copied, l * (QT - 1) + t + 1)
                    else:
                        pe.wait_ge(pt_last, l + 1)
                    if t:
                        pe.wait_ge(o_copied, l * QT + t)
                    pt = probsT[t % 2].rearrange("p (s q) -> p s q", s=NQ)
                    o4 = bank(6).rearrange("p (j q) -> p j q", j=AT)
                    for kv in range(NKV):
                        for half in range(2):
                            for odd in range(2):
                                last = mm(o4[HD * odd:HD * (odd + 1), 2 * kv:2 * kv + 2,
                                             half * CHUNK:(half + 1) * CHUNK],
                                          vw[:, 2 * t + half, kv * HD:(kv + 1) * HD],
                                          pt[:, 4 * odd + 2 * kv:4 * odd + 2 * kv + 2,
                                             half * CHUNK:(half + 1) * CHUNK], True, True)
                    last.then_inc(o_mm, 1)

                for i, kind in enumerate(PROJ):
                    n = B + i
                    pe.wait_ge(w_lo, n + 1)
                    if i >= 2:
                        pe.wait_ge(*proj_release(l, i - 2))
                    k0 = 0 if l == 0 else conv_no(l - 1, 2)
                    ready = (lambda kt: (hi_ready, k0 + kt + 1, *lo_part(k0, kt))) if i == 0 else None
                    tile_products(bank(i % 2), n % 2, hH, hL, ready)
                    if 1 <= i <= LT:
                        gates(i - 1)
                    first_g = NPROJ - LT
                    if i == first_g - 1:
                        scores_mm(0)
                    if i == first_g:
                        values()
                        scores_mm(1)
                    if i == first_g + 1:
                        probs_transposed(0)
                        scores_mm(2)
                    if i == first_g + 2:
                        outputs_mm(0)
                        probs_transposed(1)
                        scores_mm(3)
                    if i == first_g + 3:
                        outputs_mm(1)
                        probs_transposed(2)
                        pe.wait_ge(mod_done, 3 if l == 0 else 11)
                        keep_clock(12, bank(7)[:, P:2 * P])
                        outputs_mm(2)
                        probs_transposed(3)
                        keep_clock(5, bank(7)[:, P:2 * P])
                        outputs_mm(3)
                    if i in MOD_AT[l]:
                        mod_sum(MOD_AT[l][i], norm_no(l, 0))
                mods = 3 if l == 0 else 11
                norm_cols(norm_no(l, 0), mods, l)
                norm_spread(norm_no(l, 0), RB_BANK[0], 2)
                for j in range(NOUT):
                    n = B + NPROJ + j
                    pe.wait_ge(w_lo, n + 1)
                    if j < 2:
                        pe.wait_ge(*proj_release(l, NPROJ - 2 + j))
                    else:
                        pe.wait_ge(out_copied, l * NOUT + j - 1)
                    k0 = conv_no(l, 0)
                    ready = (lambda kt: (hi_ready, k0 + kt + 1, *lo_part(k0, kt))) if j == 0 else None
                    tile_products(bank(j % 2), n % 2, mH, mL, ready)
                    if NPROJ + j in MOD_AT[l]:
                        mod_sum(MOD_AT[l][NPROJ + j], norm_no(l, 1))
                mods = 5 if l == 0 else 12
                norm_cols(norm_no(l, 1), 0)
                norm_spread(norm_no(l, 1), RB_BANK[1])
                x_sum(norm_no(l, 2), mods)
                norm_spread(norm_no(l, 2), RB_BANK[2])
                for g in range(GROUPS):
                    G = B + NPROJ + NOUT + g * GSTEP
                    U = l * 2 * PAIRS + g * 2 * KT
                    with pe.Fori(0, 2) as it:
                        for c in range(8):
                            pe.wait_ge(w_lo, it * 8 + (G + c + 1))
                            pe.wait_ge(f_taps, it * 8 + (U + c + 1))
                            k0 = conv_no(l, 1)
                            ready = (lambda kt: (hi_ready, k0 + kt + 1, *lo_part(k0, kt))) if c == 0 else None
                            tile_products(bank(c % 4), c % 2, hH, hL, ready)
                        if l == 0:
                            mod_sum(it + (NMOD - 1 + 2 * g), norm_no(l, 3))
                    DN = l * GROUPS * KT + g * KT
                    VD = G + 2 * KT
                    with pe.Fori(0, KT // 2) as it:
                        for c in range(2):
                            pe.wait_ge(w_lo, it * 2 + (VD + c + 1))
                            pe.wait_ge(dn_read, it * 2 + (DN + c + 1))
                            k1 = l * PAIRS + g * KT + 1
                            ready = (lambda kt: (act_hi, k1 + kt, act_lo, k1 + kt)) if c == 0 else None
                            tile_products(bank(4 + c), c, mH, mL, ready)
                mods = 11 if l == 0 else 12
                norm_cols(norm_no(l, 3), mods)
                norm_spread(norm_no(l, 3), RB_BANK[3])
                if l + 1 < DEPTH:
                    x_sum(norm_no(l, 4), mods)
                    norm_spread(norm_no(l, 4), RB_BANK[4])


def columns(a):
    a = np.asarray(a)
    return np.swapaxes(a.reshape(*a.shape[:-1], a.shape[-1] // P, P), -1, -2)


def kernel(**inputs):
    import concourse.bacc as bacc
    from concourse.bass_utils import run_bass_kernel_spmd

    a = {k: np.asarray(v) for k, v in inputs.items()}
    L = DEPTH

    def tiles(w, n_k):
        w = w.reshape(n_k, P, w.shape[1] // P, P)
        return w.transpose(2, 1, 0, 3)
    stream = np.empty((L, NCH, P, KT, P), np.float32)
    kv = NKV * HD
    starts = {"q": 0, "k": D_ATTN, "v": D_ATTN + kv, "x": D_ATTN + 2 * kv, "g": D_ATTN + 2 * kv + D_LRU}
    for l in range(L):
        w_in = tiles(a["w_in"][l], KT)
        seen = dict.fromkeys(starts, 0)
        for i, kind in enumerate(PROJ):
            stream[l, i] = w_in[starts[kind] // P + seen[kind]]
            seen[kind] += 1
        stream[l, NPROJ:NPROJ + NOUT] = tiles(a["w_out"][l], KT)
        up = tiles(a["ffn_w_up"][l], KT)
        down = tiles(a["ffn_w_down"][l], PAIRS)
        at = NPROJ + NOUT
        for g in range(GROUPS):
            for i in range(KT):
                stream[l, at] = up[g * KT + i]
                stream[l, at + 1] = up[PAIRS + g * KT + i]
                at += 2
            stream[l, at:at + KT] = down[:, :, g * KT:(g + 1) * KT, :]
            at += KT
    stream = stream.reshape(L * NCH, P, KT * P)

    ada = a["ada_w"].reshape(L, KT, P, NMOD, D).transpose(0, 3, 1, 2, 4)
    ada = np.ascontiguousarray(ada).reshape(L * NMOD * KT, P, D)

    gw = np.zeros((L, P, 2 * LT, P), np.float32)
    for which, name in enumerate(("lru_w_a", "lru_w_x")):
        w = a[name]
        for j in range(LT):
            for b in range(2):
                s = slice(b * 64, b * 64 + 64)
                gw[:, s, which * LT + j, s] = w[:, 2 * j + b]

    par = np.empty((L, P, NPAR), np.float32)

    def put(name, cols):
        par[:, :, COLS[name]:COLS[name] + cols.shape[-1]] = cols
    for name, key in [("mix_pre", "mix_pre_g"), ("mix_post", "mix_post_g"), ("ffn_pre", "ffn_pre_g"),
                      ("ffn_post", "ffn_post_g"), ("g_attn", "grp_g_attn"), ("g_lru", "grp_g_lru"),
                      ("lcb", "lru_conv_b"), ("ba", "lru_b_a"), ("bx", "lru_b_x"), ("lam", "lru_lambda"),
                      ("fcb", "ffn_conv_b"), ("ada_b", "ada_b")]:
        put(name, columns(a[key]))
    put("lcw", columns(a["lru_conv_w"].reshape(L, CONVW * D_LRU)))
    put("fcw", columns(a["ffn_conv_w"].reshape(L, FCONV * 2 * DFF)))
    put("sink", np.broadcast_to(a["attn_sinks"][:, None, SLOTS], (L, P, NQ)))

    half = HD // 2
    inv = (THETA ** (-np.arange(0, HD, 2, dtype=np.float64) / HD)).astype(np.float32)
    arrays = {
        "in_w": stream, "in_ada": ada, "in_gw": gw, "in_par": par,
        "in_x": np.ascontiguousarray(a["x"][0].reshape(SEQ, KT, P).transpose(2, 1, 0)).reshape(P, KT * SEQ),
        "in_c": np.ascontiguousarray(columns(a["c"][0])),
        "in_pos": np.ascontiguousarray(np.broadcast_to(a["positions"][0][None, :], (P, SEQ))),
        "in_inv_freq": np.tile(inv, P // half).reshape(P, 1),
    }
    nc = bacc.Bacc("TRN2", target_bir_lowering=False, num_devices=1)
    A = {}
    for name, arr in arrays.items():
        A[name[3:]] = nc.dram_tensor(name, arr.shape, mybir.dt.from_np(arr.dtype), kind="ExternalInput").ap()
    A["out"] = nc.dram_tensor("out_0", (P, KT * SEQ), mybir.dt.float32, kind="ExternalOutput").ap()
    build(nc, A)
    r = run_bass_kernel_spmd(nc, [arrays], core_ids=[0])
    out = r.results[0]["out_0"]
    return np.ascontiguousarray(out.reshape(P, KT, SEQ).transpose(2, 1, 0)).reshape(1, SEQ, D)
```
